# Optimizing a Trainium2 kernel written in Bass

```python
import math
import jax, jax.numpy as jnp
from jax import lax
import numpy as np

D_MODEL = 1024
BATCH = 1
SEQ = 512
DEPTH = 2

N_MIXERS = 2
N_A = (DEPTH + 1) // 2
N_B = DEPTH // 2
MLA_HEADS = 16
MLA_Q_RANK = 512
MLA_KV_RANK = 256
MLA_NOPE = 64
MLA_ROPE = 32
MLA_V = 64
MLA_IN = MLA_Q_RANK + MLA_KV_RANK + MLA_ROPE
DSA_HEADS = 16
DSA_KV_HEADS = 4
DSA_GROUP = DSA_HEADS // DSA_KV_HEADS
DSA_HEAD_DIM = 64
IDX_HEADS = 8
IDX_DIM = 64
TOPK_MAX = 256
DSA_IN = (DSA_HEADS * DSA_HEAD_DIM + 2 * DSA_KV_HEADS * DSA_HEAD_DIM
          + IDX_HEADS * IDX_DIM + IDX_DIM + IDX_HEADS)
MEM_LEN = 256
XA_HEADS = 4
XA_HEAD_DIM = D_MODEL // XA_HEADS
FFN_HIDDEN = -(-8 * D_MODEL // (3 * 256)) * 256
REL_BUCKETS = 32
REL_MAX_DIST = 128
Q_BLOCK = 128
ROPE_BASE = 10000.0
LN_EPS = 1e-5
RMS_EPS = 1e-6
ALPHA = (2 * DEPTH) ** 0.25
BETA = (8 * DEPTH) ** -0.25


def layer_norm(x, g, b):
    x32 = x.astype(jnp.float32)
    mu = jnp.mean(x32, axis=-1, keepdims=True)
    var = jnp.mean(jnp.square(x32 - mu), axis=-1, keepdims=True)
    y = (x32 - mu) * lax.rsqrt(var + LN_EPS) * g.astype(jnp.float32) + b.astype(jnp.float32)
    return y.astype(x.dtype)

def rms_norm(x, g):
    x32 = x.astype(jnp.float32)
    y = x32 * lax.rsqrt(jnp.mean(jnp.square(x32), axis=-1, keepdims=True) + RMS_EPS)
    return (y * g.astype(jnp.float32)).astype(x.dtype)

def apply_rope(x, pos):
    r = x.shape[-1]
    inv_freq = ROPE_BASE ** (-jnp.arange(0, r, 2, dtype=jnp.float32) / r)
    ang = pos.astype(jnp.float32)[..., None] * inv_freq
    cos = jnp.cos(ang)[:, :, None, :]
    sin = jnp.sin(ang)[:, :, None, :]
    x32 = x.astype(jnp.float32)
    x1, x2 = x32[..., : r // 2], x32[..., r // 2:]
    out = jnp.concatenate([x1 * cos - x2 * sin, x1 * sin + x2 * cos], axis=-1)
    return out.astype(x.dtype)

def t5_bucket(dist):
    max_exact = REL_BUCKETS // 2
    n = jnp.maximum(dist, 0)
    nf = jnp.maximum(n, 1).astype(jnp.float32)
    large = max_exact + (jnp.log(nf / max_exact) / math.log(REL_MAX_DIST / max_exact)
                         * (REL_BUCKETS - max_exact)).astype(jnp.int32)
    large = jnp.minimum(large, REL_BUCKETS - 1)
    return jnp.where(n < max_exact, n, large)

def to_blocks(a, nb):
    return jnp.moveaxis(a.reshape(a.shape[0], nb, Q_BLOCK, *a.shape[2:]), 1, 0)

def from_blocks(a):
    a = jnp.moveaxis(a, 0, 1)
    return a.reshape(a.shape[0], a.shape[1] * a.shape[2], *a.shape[3:])

gather_rows = jax.vmap(lambda table, idx: table[idx])

def dense_causal_attention(q, k, v, scale):
    s_len = q.shape[1]
    nb = s_len // Q_BLOCK
    key_idx = jnp.arange(s_len)

    def one_block(args):
        q_blk, start = args
        logits = jnp.einsum('bqhd,bkhd->bhqk', q_blk, k).astype(jnp.float32) * scale
        q_idx = start + jnp.arange(Q_BLOCK)
        causal = key_idx[None, :] <= q_idx[:, None]
        logits = jnp.where(causal[None, None], logits, -jnp.inf)
        p = jax.nn.softmax(logits, axis=-1).astype(v.dtype)
        return jnp.einsum('bhqk,bkhd->bqhd', p, v)

    out = lax.map(one_block, (to_blocks(q, nb), jnp.arange(nb) * Q_BLOCK))
    return from_blocks(out)

def mla_mixer(x, pos, w_in, q_norm, w_uq, kv_norm, w_ukv, w_o):
    b, s, _ = x.shape
    h = x @ w_in
    c_q = h[..., :MLA_Q_RANK]
    c_kv = h[..., MLA_Q_RANK:MLA_Q_RANK + MLA_KV_RANK]
    k_rope = h[..., MLA_Q_RANK + MLA_KV_RANK:]
    q = (rms_norm(c_q, q_norm) @ w_uq).reshape(b, s, MLA_HEADS, MLA_NOPE + MLA_ROPE)
    q = jnp.concatenate([q[..., :MLA_NOPE], apply_rope(q[..., MLA_NOPE:], pos)], axis=-1)
    kv = (rms_norm(c_kv, kv_norm) @ w_ukv).reshape(b, s, MLA_HEADS, MLA_NOPE + MLA_V)
    k_nope, v = kv[..., :MLA_NOPE], kv[..., MLA_NOPE:]
    k_rope = apply_rope(k_rope[:, :, None, :], pos)
    k = jnp.concatenate([k_nope, jnp.broadcast_to(k_rope, (b, s, MLA_HEADS, MLA_ROPE))], axis=-1)
    out = dense_causal_attention(q, k, v, (MLA_NOPE + MLA_ROPE) ** -0.5)
    return out.reshape(b, s, MLA_HEADS * MLA_V) @ w_o

def dsa_mixer(x, pos, rel_bias, w_in, w_o):
    b, s, _ = x.shape
    nb = s // Q_BLOCK
    topk = min(TOPK_MAX, s // 4)
    h = x @ w_in
    o1 = DSA_HEADS * DSA_HEAD_DIM
    o2 = o1 + DSA_KV_HEADS * DSA_HEAD_DIM
    o3 = o2 + DSA_KV_HEADS * DSA_HEAD_DIM
    o4 = o3 + IDX_HEADS * IDX_DIM
    o5 = o4 + IDX_DIM
    q = h[..., :o1].reshape(b, s, DSA_HEADS, DSA_HEAD_DIM)
    k = h[..., o1:o2].reshape(b, s, DSA_KV_HEADS, DSA_HEAD_DIM)
    v = h[..., o2:o3].reshape(b, s, DSA_KV_HEADS, DSA_HEAD_DIM)
    q_idx = h[..., o3:o4].reshape(b, s, IDX_HEADS, IDX_DIM)
    k_idx = h[..., o4:o5]
    w_idx = h[..., o5:] * (IDX_HEADS ** -0.5)
    key_idx = jnp.arange(s)

    def one_block(args):
        q_blk, qi_blk, wi_blk, pos_blk, start = args
        t_idx = start + jnp.arange(Q_BLOCK)
        causal = key_idx[None, :] <= t_idx[:, None]
        dots = jnp.einsum('bqhd,bkd->bqhk', qi_blk, k_idx).astype(jnp.float32) * (IDX_DIM ** -0.5)
        score = jnp.einsum('bqh,bqhk->bqk', wi_blk.astype(jnp.float32), jax.nn.relu(dots))
        score = jnp.where(causal[None], score, -jnp.inf)
        _, sel = lax.top_k(score, topk)
        sel_ok = sel <= t_idx[None, :, None]
        k_sel = gather_rows(k, sel)
        v_sel = gather_rows(v, sel)
        pos_sel = gather_rows(pos, sel)
        qg = q_blk.reshape(b, Q_BLOCK, DSA_KV_HEADS, DSA_GROUP, DSA_HEAD_DIM)
        logits = jnp.einsum('bqngd,bqknd->bqngk', qg, k_sel).astype(jnp.float32) * (DSA_HEAD_DIM ** -0.5)
        bucket = t5_bucket(pos_blk[:, :, None] - pos_sel)
        bias = rel_bias[bucket].astype(jnp.float32)
        bias = bias.reshape(b, Q_BLOCK, topk, DSA_KV_HEADS, DSA_GROUP).transpose(0, 1, 3, 4, 2)
        logits = jnp.where(sel_ok[:, :, None, None, :], logits + bias, -jnp.inf)
        p = jax.nn.softmax(logits, axis=-1).astype(v.dtype)
        o = jnp.einsum('bqngk,bqknd->bqngd', p, v_sel)
        return o.reshape(b, Q_BLOCK, DSA_HEADS * DSA_HEAD_DIM)

    out = lax.map(one_block, (to_blocks(q, nb), to_blocks(q_idx, nb), to_blocks(w_idx, nb),
                              to_blocks(pos, nb), jnp.arange(nb) * Q_BLOCK))
    return from_blocks(out) @ w_o

def memory_cross_attention(x, mem, w_q, w_kv, w_o):
    b, s, _ = x.shape
    m = mem.shape[1]
    q = (x @ w_q).reshape(b, s, XA_HEADS, XA_HEAD_DIM)
    kv = (mem @ w_kv).reshape(b, m, 2, XA_HEADS, XA_HEAD_DIM)
    k, v = kv[:, :, 0], kv[:, :, 1]
    logits = jnp.einsum('bshd,bmhd->bhsm', q, k).astype(jnp.float32) * (XA_HEAD_DIM ** -0.5)
    p = jax.nn.softmax(logits, axis=-1).astype(v.dtype)
    o = jnp.einsum('bhsm,bmhd->bshd', p, v)
    return o.reshape(b, s, D_MODEL) @ w_o

def swiglu_ffn(x, w_in, w_down):
    h = x @ w_in
    g, u = h[..., :FFN_HIDDEN], h[..., FFN_HIDDEN:]
    return (jax.nn.silu(g) * u) @ w_down

def first_inputs(seed: int = 0) -> dict:
    key = jax.random.key(seed)
    ks = jax.random.split(key, 24)
    f32 = jnp.float32

    def w(k, shape, fan_in, scale=1.0):
        return jax.random.normal(k, shape, f32) * (fan_in ** -0.5) * scale

    x = jax.random.normal(ks[0], (BATCH, SEQ, D_MODEL), f32)
    mem = jax.random.normal(ks[1], (BATCH, MEM_LEN, D_MODEL), f32)
    offset = jax.random.randint(ks[2], (BATCH, 1), 0, 1024, dtype=jnp.int32)
    positions = (offset + jnp.arange(SEQ, dtype=jnp.int32)[None, :]).astype(jnp.int32)
    rel_bias = jax.random.normal(ks[3], (REL_BUCKETS, DSA_HEADS), f32) * 0.5
    return {
        "x": x,
        "mem": mem,
        "positions": positions,
        "rel_bias": rel_bias,
        "mla_w_in": w(ks[4], (N_A, D_MODEL, MLA_IN), D_MODEL),
        "mla_q_norm": 1.0 + 0.01 * jax.random.normal(ks[5], (N_A, MLA_Q_RANK), f32),
        "mla_w_uq": w(ks[6], (N_A, MLA_Q_RANK, MLA_HEADS * (MLA_NOPE + MLA_ROPE)), MLA_Q_RANK),
        "mla_kv_norm": 1.0 + 0.01 * jax.random.normal(ks[7], (N_A, MLA_KV_RANK), f32),
        "mla_w_ukv": w(ks[8], (N_A, MLA_KV_RANK, MLA_HEADS * (MLA_NOPE + MLA_V)), MLA_KV_RANK),
        "mla_w_o": w(ks[9], (N_A, MLA_HEADS * MLA_V, D_MODEL), MLA_HEADS * MLA_V, BETA),
        "dsa_w_in": w(ks[10], (N_B, D_MODEL, DSA_IN), D_MODEL),
        "dsa_w_o": w(ks[11], (N_B, DSA_HEADS * DSA_HEAD_DIM, D_MODEL), DSA_HEADS * DSA_HEAD_DIM, BETA),
        "xa_w_q": w(ks[12], (DEPTH, D_MODEL, D_MODEL), D_MODEL),
        "xa_w_kv": w(ks[13], (DEPTH, D_MODEL, 2 * D_MODEL), D_MODEL),
        "xa_w_o": w(ks[14], (DEPTH, D_MODEL, D_MODEL), D_MODEL, BETA),
        "ffn_w_in": w(ks[15], (DEPTH, D_MODEL, 2 * FFN_HIDDEN), D_MODEL),
        "ffn_w_down": w(ks[16], (DEPTH, FFN_HIDDEN, D_MODEL), FFN_HIDDEN, BETA),
        "ln_g": 1.0 + 0.01 * jax.random.normal(ks[17], (DEPTH, 3, D_MODEL), f32),
        "ln_b": 0.01 * jax.random.normal(ks[18], (DEPTH, 3, D_MODEL), f32),
    }

def first_block(x, mem, positions, rel_bias, mla_w_in, mla_q_norm, mla_w_uq, mla_kv_norm,
              mla_w_ukv, mla_w_o, dsa_w_in, dsa_w_o, xa_w_q, xa_w_kv, xa_w_o,
              ffn_w_in, ffn_w_down, ln_g, ln_b):
    for i in range(DEPTH):
        j = i // N_MIXERS
        if i % N_MIXERS == 0:
            y = mla_mixer(x, positions, mla_w_in[j], mla_q_norm[j], mla_w_uq[j],
                          mla_kv_norm[j], mla_w_ukv[j], mla_w_o[j])
        else:
            y = dsa_mixer(x, positions, rel_bias, dsa_w_in[j], dsa_w_o[j])
        x = layer_norm(ALPHA * x + y, ln_g[i, 0], ln_b[i, 0])
        y = memory_cross_attention(x, mem, xa_w_q[i], xa_w_kv[i], xa_w_o[i])
        x = layer_norm(ALPHA * x + y, ln_g[i, 1], ln_b[i, 1])
        y = swiglu_ffn(x, ffn_w_in[i], ffn_w_down[i])
        x = layer_norm(ALPHA * x + y, ln_g[i, 2], ln_b[i, 2])
    return x


DEPTH_2 = 1

ATTN_W = D_MODEL // 2
N_ATTN_HEADS = 8
HEAD_DIM = ATTN_W // N_ATTN_HEADS
POOL_W = D_MODEL - ATTN_W
POOL_WINDOWS = (2, 4, 8, 16)
POOL_C = POOL_W // len(POOL_WINDOWS)
IN_COLS = 3 * ATTN_W + N_ATTN_HEADS + POOL_W
D_FF = 2816
CONV_W = 3
EPS = 1e-6


def _rmsnorm(x, g):
    x32 = x.astype(jnp.float32)
    y = x32 * lax.rsqrt(jnp.mean(x32 * x32, axis=-1, keepdims=True) + EPS)
    return (y * g.astype(jnp.float32)).astype(x.dtype)

def _fox_attention(q, k, v, log_f):
    B, S, H, Dh = q.shape
    nb = S // Q_BLOCK
    F = jnp.cumsum(log_f, axis=1)
    Fk = F.transpose(0, 2, 1)
    q32 = q.astype(jnp.float32) * (Dh ** -0.5)
    k32 = k.astype(jnp.float32)
    v32 = v.astype(jnp.float32)
    qb = q32.reshape(B, nb, Q_BLOCK, H, Dh).transpose(1, 0, 2, 3, 4)
    Fq = F.reshape(B, nb, Q_BLOCK, H).transpose(1, 0, 3, 2)
    kpos = jnp.arange(S)

    def one_block(args):
        i, qi, Fi = args
        s = jnp.einsum('bqhd,bkhd->bhqk', qi, k32)
        s = s + Fi[..., None] - Fk[:, :, None, :]
        qpos = i * Q_BLOCK + jnp.arange(Q_BLOCK)
        s = jnp.where(qpos[:, None] >= kpos[None, :], s, -jnp.inf)
        p = jax.nn.softmax(s, axis=-1)
        return jnp.einsum('bhqk,bkhd->bqhd', p, v32)

    o = lax.map(one_block, (jnp.arange(nb), qb, Fq))
    return o.transpose(1, 0, 2, 3, 4).reshape(B, S, H * Dh)

def _multiscale_pool(u, pool_w, pool_scale):
    B, S, _ = u.shape
    u32 = u.astype(jnp.float32)
    count = jnp.arange(1, S + 1, dtype=jnp.float32)
    outs = []
    for g, w in enumerate(POOL_WINDOWS):
        ug = u32[..., g * POOL_C:(g + 1) * POOL_C]
        csp = jnp.concatenate([jnp.zeros((B, 1, POOL_C), jnp.float32),
                               jnp.cumsum(ug, axis=1)], axis=1)
        lo = jnp.concatenate([jnp.zeros((B, w - 1, POOL_C), jnp.float32),
                              csp[:, :S - w + 1]], axis=1)
        mean = (csp[:, 1:] - lo) / jnp.minimum(count, w)[None, :, None]
        outs.append(jnp.einsum('bsc,cd->bsd', mean - ug, pool_w[g].astype(jnp.float32)))
    out = jnp.concatenate(outs, axis=-1) * pool_scale.astype(jnp.float32)
    return out.astype(u.dtype)

def _conv_ffn(h, w_up, conv_w, conv_b, w_down):
    S = h.shape[1]
    a = h @ w_up
    ap = jnp.pad(a, ((0, 0), (CONV_W - 1, 0), (0, 0)))
    conv = conv_b + ap[:, 0:S] * conv_w[0]
    for j in range(1, CONV_W):
        conv = conv + ap[:, j:j + S] * conv_w[j]
    gate, val = jnp.split(conv, 2, axis=-1)
    return (jax.nn.silu(gate) * val) @ w_down

def second_inputs(seed: int = 0) -> dict:
    key = jax.random.key(seed)
    ks = jax.random.split(key, 18)
    f32 = jnp.float32
    nrm = lambda k, shape, s: jax.random.normal(k, shape, f32) * s
    return {
        "x": nrm(ks[0], (BATCH, SEQ, D_MODEL), 1.0),
        "c": nrm(ks[1], (BATCH, D_MODEL), 1.0),
        "mod_w": nrm(ks[2], (DEPTH_2, D_MODEL, 6 * D_MODEL), 0.5 * D_MODEL ** -0.5),
        "mod_b": nrm(ks[3], (DEPTH_2, 6 * D_MODEL), 0.02),
        "norm1_g": 1.0 + nrm(ks[4], (DEPTH_2, D_MODEL), 0.02),
        "norm2_g": 1.0 + nrm(ks[5], (DEPTH_2, D_MODEL), 0.02),
        "w_in": nrm(ks[6], (DEPTH_2, D_MODEL, IN_COLS), D_MODEL ** -0.5),
        "b_f": jax.random.uniform(ks[7], (DEPTH_2, N_ATTN_HEADS), f32, 1.0, 6.0),
        "pool_w": nrm(ks[8], (DEPTH_2, len(POOL_WINDOWS), POOL_C, POOL_C), POOL_C ** -0.5),
        "pool_scale": 1.0 + nrm(ks[9], (DEPTH_2, POOL_W), 0.1),
        "w_out": nrm(ks[10], (DEPTH_2, ATTN_W + POOL_W, D_MODEL), (ATTN_W + POOL_W) ** -0.5),
        "ffn_up": nrm(ks[11], (DEPTH_2, D_MODEL, 2 * D_FF), D_MODEL ** -0.5),
        "ffn_conv_w": nrm(ks[12], (DEPTH_2, CONV_W, 2 * D_FF), CONV_W ** -0.5),
        "ffn_conv_b": nrm(ks[13], (DEPTH_2, 2 * D_FF), 0.02),
        "ffn_down": nrm(ks[14], (DEPTH_2, D_FF, D_MODEL), D_FF ** -0.5),
        "final_g": 1.0 + nrm(ks[15], (D_MODEL,), 0.02),
    }

def second_block(x, c, mod_w, mod_b, norm1_g, norm2_g, w_in, b_f, pool_w, pool_scale,
              w_out, ffn_up, ffn_conv_w, ffn_conv_b, ffn_down, final_g):
    B, S, _ = x.shape
    c_act = jax.nn.silu(c)
    splits = [ATTN_W, 2 * ATTN_W, 3 * ATTN_W, 3 * ATTN_W + N_ATTN_HEADS]
    for l in range(DEPTH_2):
        mod = (c_act @ mod_w[l] + mod_b[l])[:, None, :]
        sh1, sc1, g1, sh2, sc2, g2 = jnp.split(mod, 6, axis=-1)

        h = _rmsnorm(x, norm1_g[l]) * (1.0 + sc1) + sh1
        z = h @ w_in[l]
        q, k, v, f_logit, u = jnp.split(z, splits, axis=-1)
        log_f = jax.nn.log_sigmoid((f_logit + b_f[l]).astype(jnp.float32))
        hd = (B, S, N_ATTN_HEADS, HEAD_DIM)
        attn = _fox_attention(q.reshape(hd), k.reshape(hd), v.reshape(hd), log_f)
        pool = _multiscale_pool(u, pool_w[l], pool_scale[l])
        mixed = jnp.concatenate([attn.astype(x.dtype), pool], axis=-1)
        x = x + g1 * (mixed @ w_out[l])

        h = _rmsnorm(x, norm2_g[l]) * (1.0 + sc2) + sh2
        x = x + g2 * _conv_ffn(h, ffn_up[l], ffn_conv_w[l], ffn_conv_b[l], ffn_down[l])
    return _rmsnorm(x, final_g)


def setup_inputs(seed=0):
    out = dict(first_inputs(seed))
    for name, value in second_inputs(seed + 1).items():
        if name != "x":
            out[name + "_2"] = value
    return out


def reference(
    x, mem, positions, rel_bias, mla_w_in, mla_q_norm, mla_w_uq, mla_kv_norm, mla_w_ukv,
    mla_w_o, dsa_w_in, dsa_w_o, xa_w_q, xa_w_kv, xa_w_o, ffn_w_in, ffn_w_down, ln_g, ln_b, c_2,
    mod_w_2, mod_b_2, norm1_g_2, norm2_g_2, w_in_2, b_f_2, pool_w_2, pool_scale_2, w_out_2,
    ffn_up_2, ffn_conv_w_2, ffn_conv_b_2, ffn_down_2, final_g_2,
):
    x = first_block(
        x, mem, positions, rel_bias, mla_w_in, mla_q_norm, mla_w_uq, mla_kv_norm, mla_w_ukv,
        mla_w_o, dsa_w_in, dsa_w_o, xa_w_q, xa_w_kv, xa_w_o, ffn_w_in, ffn_w_down, ln_g, ln_b,
    )
    return second_block(
        x, c_2, mod_w_2, mod_b_2, norm1_g_2, norm2_g_2, w_in_2, b_f_2, pool_w_2, pool_scale_2,
        w_out_2, ffn_up_2, ffn_conv_w_2, ffn_conv_b_2, ffn_down_2, final_g_2,
    )


_drawn_inputs = setup_inputs


def setup_inputs(seed=0):
    import zlib

    import numpy as np

    out = dict(_drawn_inputs(seed))
    spreads = {}
    factors = {'mla_q_norm': 8.0,
     'mla_kv_norm': 8.0,
     'norm1_g_2': 8.0,
     'norm2_g_2': 8.0,
     'pool_scale_2': 3.237,
     'ffn_conv_b_2': 8.0,
     'final_g_2': 2.878}
    for name, (base, spread) in spreads.items():
        noise = np.random.default_rng([zlib.crc32(name.encode()), seed]).standard_normal(out[name].shape)
        drawn = base * np.exp(spread * noise) if base else spread * noise
        out[name] = __import__('jax').numpy.asarray(drawn.astype(out[name].dtype))
    for name, factor in factors.items():
        out[name] = (out[name] * factor).astype(out[name].dtype)
    return out
```

```python
from contextlib import ExitStack

import numpy as np
import concourse.bass as bass
from concourse import mybir

ALU = mybir.AluOpType
ACT = mybir.ActivationFunctionType
F32 = mybir.dt.float32
F32R = mybir.dt.float32r
BF16 = mybir.dt.bfloat16
I32 = mybir.dt.int32

P = 128
S, D, MEM = 512, 1024, 256
DC = D // P
NQ = S // P
DEPTH = 2
ALPHA = (2 * DEPTH) ** 0.25
LN_EPS, RMS_EPS = 1e-5, 1e-6
QRANK, KVRANK, NOPE, ROPE, HEADS = 512, 256, 64, 32, 16
MLA_SCALE = (NOPE + ROPE) ** -0.5
FF = 2816
FC = FF // P
TOPK = 128
BUCKETS, REL_MAX = 32, 128
IDXH = 8
FOXH = 8
WINDOWS = (2, 4, 8, 16)
NEG = -1.0e30
TAKEN = -3.0e38

UW = 2048
STAGES = [
    ("x_in", 0, 8), ("mla_in", 4, 7), ("mla_uq", 4, 12), ("mla_ukv", 2, 16), ("mla_o", 4, 8),
    ("mem0", 0, 8), ("xa_kv0", 8, 16), ("xa_q0", 4, 8), ("xa_o0", 4, 8),
    ("ffn_in0", 22, 44), ("ffn_down0", 11, 0),
    ("dsa_q", 4, 8), ("dsa_k", 1, 6), ("dsa_v", 1, 4), ("dsa_qi", 2, 4), ("dsa_ki", 1, 6), ("dsa_o", 4, 8),
    ("mem1", 0, 8), ("xa_kv1", 8, 16), ("xa_q1", 4, 8), ("xa_o1", 4, 8),
    ("ffn_in1", 22, 44), ("ffn_down1", 11, 0),
    ("mod", 24, 24),
    ("fox_qk", 4, 8), ("fox_v", 2, 8), ("fox_f", 1, 1), ("fox_u", 2, 4), ("fox_pool", 1, 4), ("fox_o", 4, 8),
    ("ffn_in2", 22, 44), ("ffn_down2", 11, 0),
]
UNIT0, TILE0, UNITS, TILES = {}, {}, {}, {}
_u, _t = 0, 4
for _name, _nu, _nt in STAGES:
    UNIT0[_name], TILE0[_name], UNITS[_name], TILES[_name] = _u, _t, _nu, _nt
    _u, _t = _u + _nu, _t + _nt
N_UNITS = _u
LOADS = {"mla_uq": 8, "mla_ukv": 4}
LOADED = []
for _name, _nu, _ in STAGES:
    for _ in range(_nu):
        LOADED.append((LOADED[-2] if len(LOADED) > 1 else 0) + 16 * LOADS.get(_name, 2))

STEP0 = {"mla": 4, "xa0": 68, "dsa": 84, "xa1": 148, "fox": 164}
FILLS = ["x0", "mla_o", "ln0", "xa0_o", "ln1", "ln2", "dsa_o", "ln3", "xa1_o", "ln4", "rms1", "fox_o", "rms2"]
FILL0 = {n: 8 * i for i, n in enumerate(FILLS)}
NORMS = ["ln0", "ln1", "ln2", "ln3", "ln4", "ln5", "rms1", "rms2", "rms3"]
NORM_I = {n: i for i, n in enumerate(NORMS)}

COLS = {}
_c = 0
for _name, _n in (("ln_g", 48), ("ln_b", 48), ("q_norm", 4), ("kv_norm", 2), ("norm1", 8), ("norm2", 8), ("final", 8)):
    COLS[_name] = _c
    _c += _n
_c = 128
for _name, _n in (("pool_scale", 4), ("conv_b", 44), ("mod_b", 48), ("c", 8)):
    COLS[_name] = _c
    _c += _n
COLS["conv_w0"], COLS["conv_w1"], COLS["conv_w2"] = 256, 300, 384

K_ID, K_PERM, K_ONES, K_CM, K_CNT = 0, 128, 256, 384, 896
K_FREQ, K_THR = 960, 961
K_SEL = 968
K_N = 1224
K_REP, K_ROT = 1224, 1352
K_ALL = 1480


def shape_constants():
    k = np.zeros((P, K_ALL), np.float32)
    p = np.arange(P)
    k[:, K_ID:K_ID + P] = np.eye(P)
    for m in range(P):
        low = m % ROPE < ROPE // 2
        k[m + ROPE // 2 if low else m - ROPE // 2, K_PERM + m] = -1.0 if low else 1.0
    for m in range(P):
        r = m % ROPE
        k[P - ROPE + r, K_REP + m] = 1.0
        k[P - ROPE + (r + ROPE // 2) % ROPE, K_ROT + m] = -1.0 if r < ROPE // 2 else 1.0
    for half in range(2):
        k[64 * half + p % 64, K_SEL + P * half + p] = 1.0
    k[:, K_ONES:K_ONES + P] = 1.0 / D
    k[:, K_CM:K_CM + S] = np.where(np.arange(S)[None, :] - (S - P) <= p[:, None], 0.0, NEG)
    for g, w in enumerate(WINDOWS):
        k[:, K_CNT + 16 * g:K_CNT + 16 * g + 16] = 1.0 / np.minimum(np.arange(16) + 1, w)
    inv = 10000.0 ** (-np.arange(0, ROPE, 2, dtype=np.float64) / ROPE)
    k[:, K_FREQ] = inv.astype(np.float32)[p % (ROPE // 2)]
    b = np.arange(BUCKETS)
    half = BUCKETS // 2
    far = np.ceil(half * (REL_MAX / half) ** ((b - half) / half) - 1e-9)
    thr = np.where(b < half, b, far)
    thr[0] = -(2.0 ** 30)
    k[:, K_THR] = thr.astype(np.float32)[p % BUCKETS]
    return k


def build_program(nc, A, consts, out):
    ctx = ExitStack()
    with ctx:
        def sem(name):
            return ctx.enter_context(nc.semaphore(name))

        total = nc.sbuf_bytes_remaining // 64 * 64 - 64
        slab = nc.alloc_sbuf_tensor("slab", [P, total // 4], F32)
        end = nc.sbuf_base
        base = end - total
        top = [base]

        def at(name, shape, offset, dt=F32):
            return nc.alloc_sbuf_tensor_at(name, shape, dt, offset=offset)

        def keep(name, shape, dt=F32):
            size = int(np.prod(shape[1:])) * (2 if dt == BF16 else 4)
            t = at(name, shape, top[0], dt)
            top[0] += -(-size // 32) * 32
            return t

        RAW = keep("RAW", [P, 2, UW])
        WH = keep("WH", [P, 2, UW], F32R)
        WL = keep("WL", [P, 2, UW], F32R)
        XT = keep("XT", [P, DC, S])
        COL = keep("COL", [P, 512])
        KC = keep("KC", [P, K_N])
        MODC = keep("MODC", [P, 48])
        MODR = keep("MODR", [P, 48])
        CA = keep("CA", [P, 8])
        CAH = keep("CAH", [P, 8], F32R)
        CAL = keep("CAL", [P, 8], F32R)
        G1 = keep("G1", [P, 8])
        G2 = keep("G2", [P, 8])
        EPS = keep("EPS", [P, 4])
        BF = keep("BF", [P, 1])
        MX = keep("MX", [P, 4])
        NM = keep("NM", [P, 4])
        RS = keep("RS", [P, 4])
        RI = keep("RI", [P, 4])
        M8 = keep("M8", [P, 8])
        WIX = keep("WIX", [P, NQ, IDXH])
        DEL = keep("DEL", [96, HEADS], BF16)
        region = top[0]
        XH = keep("XH", [P, DC, S], F32R)
        XL = keep("XL", [P, DC, S], F32R)
        arena = top[0]
        assert arena + 104 * 1024 <= end, (arena, end)
        KB = 1024

        IDN = KC[:, K_ID:K_ID + P]
        PERM = KC[:, K_PERM:K_PERM + P]
        ONES = KC[:, K_ONES:K_ONES + P]
        SEL = [KC[:, K_SEL + P * h:K_SEL + P * h + P] for h in range(2)]

        def cm(qb):
            return KC[:, K_CM + S - P - P * qb:K_CM + S]

        ZB = at("ZB", [P, DC, S], arena)
        SQ = at("SQ", [P, 4, S], arena + 16 * KB)
        STD = at("STD", [P, S], arena + 24 * KB)
        RSTD = at("RSTD", [P, S], arena + 26 * KB)
        HH = at("HH", [P, FC, S], arena, F32R)
        HL = at("HL", [P, FC, S], arena + 44 * KB, F32R)
        SG = at("SG", [P, 2, S], arena + 88 * KB)
        HF = at("HF", [P, 2, S], arena + 92 * KB)
        XN = at("XN", [P, NQ, D], arena)
        VR = at("VR", [P, 4, P], arena + 16 * KB)
        QN = at("QN", [P, 8, S], arena)
        QR = at("QR", [P, 4, S], arena + 16 * KB)
        KN = at("KN", [P, 8, S], arena + 24 * KB)
        VM = at("VM", [P, NQ, D], arena + 40 * KB)
        KR = at("KR", [P, S], arena + 56 * KB)
        COS = at("COS", [P, S], arena + 58 * KB)
        SIN = at("SIN", [P, S], arena + 60 * KB)
        CR = at("CR", [P, 6, S], arena + 62 * KB)
        CH = at("CH", [P, 6, S], arena + 74 * KB, F32R)
        CL = at("CL", [P, 6, S], arena + 86 * KB, F32R)
        MSQ = at("MSQ", [P, 4, S], arena)
        RQ = at("RQ", [P, 2, S], arena + 8 * KB)
        RT = at("RT", [P, 2, S], arena + 12 * KB)
        POSI = at("POSI", [P, S], arena + 40 * KB, I32)
        ANG = at("ANG", [P, S], arena + 42 * KB)
        TRN = at("TRN", [P, S], arena + 44 * KB)
        RP = at("RP", [P, 2, S], arena + 98 * KB)
        KRAW = at("KRAW", [P, S], arena + 38 * KB)
        KROT = at("KROT", [P, 2, P], arena + 36 * KB)
        REP, ROT = KROT[:, 0, :], KROT[:, 1, :]
        Q_M = at("Q_M", [P, 3, S], arena + 62 * KB)
        K_M = at("K_M", [P, 2, S], arena + 68 * KB)
        V_M = at("V_M", [P, NQ, 256], arena + 72 * KB)
        PB_M = at("PB_M", [P, 4, S], arena + 76 * KB)
        PT_M = at("PT_M", [P, 2, S], arena + 84 * KB)
        QX = at("QX", [P, 8, S], arena + 28 * KB)
        KX = at("KX", [P, 8, MEM], arena + 44 * KB)
        VX = at("VX", [P, 2, D], arena + 52 * KB)
        MN = at("MN", [P, 2, D], arena + 60 * KB)
        MH = at("MH", [P, DC, MEM], arena + 68 * KB, F32R)
        ML = at("ML", [P, DC, MEM], arena + 76 * KB, F32R)
        Q_X = at("Q_X", [P, 2, S], arena + 84 * KB)
        V_X = at("V_X", [P, 2, 256], arena + 88 * KB)
        PB_X = at("PB_X", [P, 4, S], arena + 90 * KB)
        PT_X = at("PT_X", [P, 2, S], arena + 98 * KB)
        QD = at("QD", [P, 8, S], arena)
        KD = at("KD", [P, 4, S], arena + 16 * KB)
        BI = at("BI", [P, HEADS, 1280], arena + 24 * KB)
        QI = at("QI", [P, 4, S], arena + 24 * KB)
        KI = at("KI", [P, S], arena + 32 * KB)
        RL = at("RL", [P, 2, S], arena + 34 * KB)
        VD = at("VD", [P, NQ, 256], arena + 40 * KB)
        PB_D = at("PB_D", [P, 4, S], region)
        PT_D = at("PT_D", [P, 2, S], region + 8 * KB)
        Q_D = at("Q_D", [P, 2, S], region + 12 * KB)
        K_D = at("K_D", [P, S], region + 16 * KB)
        V_D = at("V_D", [P, NQ, 64], region + 18 * KB)
        VK = at("VK", [P, NQ, 256], region + 19 * KB)
        MK = at("MK", [P, 1280], region + 23 * KB)
        ST = at("ST", [96, 8, S], region, BF16)
        PQ = at("PQ", [96, S], region + 8 * KB)
        PK = at("PK", [96, S], region + 10 * KB)
        PI = at("PI", [96, S], region + 12 * KB, I32)
        RB = at("RB", [96, 2, HEADS], region + 14 * KB)
        DW = at("DW", [96, 4, HEADS], region + 15 * KB)
        DB = at("DB", [96, 3, HEADS], region + 16 * KB, BF16)
        QF = at("QF", [P, 8, S], arena)
        VF = at("VF", [P, NQ, S], arena + 16 * KB)
        UF = at("UF", [P, 4, S], arena + 28 * KB)
        PLH = at("PLH", [P, 4, S], arena + 36 * KB, F32R)
        PLL = at("PLL", [P, 4, S], arena + 44 * KB, F32R)
        FB = at("FB", [P, FOXH, S], arena + 52 * KB)
        FG = at("FG", [P, 4, S], arena + 68 * KB)
        FQ = at("FQ", [P, NQ, FOXH], arena + 76 * KB)
        Q_F = at("Q_F", [P, 2, S], arena + 77 * KB)
        K_F = at("K_F", [P, 2, S], arena + 81 * KB)
        V_F = at("V_F", [P, NQ, 256], arena + 85 * KB)
        PB_F = at("PB_F", [P, 4, S], arena + 89 * KB)
        PT_F = at("PT_F", [P, 2, S], arena + 97 * KB)
        PW = at("PW", [P, 3, S], arena + 89 * KB)
        ON = at("ON", [P, NQ, D], arena + 28 * KB)

        bank = [ctx.enter_context(nc.psum_tensor(f"bank{i}", [P, 512], F32)) for i in range(8)]

        w_loaded = [sem("w_loaded0"), sem("w_loaded1")]
        w_hi = sem("w_hi")
        w_split = sem("w_split")
        tile_ready = sem("tile_ready")
        tile_free = sem("tile_free")
        unit_used = sem("unit_used")
        y_ready = sem("y_ready")
        y_free = sem("y_free")
        x_hi = sem("x_hi")
        x_split = sem("x_split")
        silu_done = sem("silu_done")
        hid_hi = sem("hid_hi")
        hid_split = sem("hid_split")
        tap_done = sem("tap_done")
        conv_acc = sem("conv_acc")
        mean_ready = sem("mean_ready")
        centred = sem("centred")
        squared = sem("squared")
        sq_summed = sem("sq_summed")
        std_done = sem("std_done")
        rstd_done = sem("rstd_done")
        scaled = sem("scaled")
        affine = sem("affine")
        small_in = sem("small_in")
        x_in = sem("x_in")
        mem_in = sem("mem_in")
        pos_in = sem("pos_in")
        cols_t = sem("cols_t")
        cols_done = sem("cols_done")
        c_hi = sem("c_hi")
        c_split = sem("c_split")
        c_scaled = sem("c_scaled")
        c_affine = sem("c_affine")
        rope_mm = sem("rope_mm")
        rope_dve = sem("rope_dve")
        trig = sem("trig")
        trig_act = sem("trig_act")
        logits_ready = sem("logits_ready")
        logits_seen = sem("logits_seen")
        max_done = sem("max_done")
        negmax_done = sem("negmax_done")
        exp_done = sem("exp_done")
        rsum_done = sem("rsum_done")
        probs_ready = sem("probs_ready")
        turned = sem("turned")
        pt_done = sem("pt_done")
        av_done = sem("av_done")
        staged = sem("staged")
        bias_staged = sem("bias_staged")
        comb_done = sem("comb_done")
        o_copied = sem("o_copied")
        idx_ready = sem("idx_ready")
        idx_relu = sem("idx_relu")
        idx_acc = sem("idx_acc")
        topk = sem("topk")
        rel_in = sem("rel_in")
        rows_in = sem("rows_in")
        gate_in = sem("gate_in")
        eps_done = sem("eps_done")
        pool_zero = sem("pool_zero")
        v_moved = sem("v_moved")
        rel_dve = sem("rel_dve")
        step_done = sem("step_done")
        step_used = sem("step_used")
        bias_ready = sem("bias_ready")
        bias_free = sem("bias_free")
        mod_done = sem("mod_done")
        mod_hi = sem("mod_hi")
        f_act = sem("f_act")
        f_dve = sem("f_dve")
        f_mm = sem("f_mm")
        pool_dve = sem("pool_dve")
        pool_hi = sem("pool_hi")
        pool_split = sem("pool_split")
        out_ready = sem("out_ready")
        stored = sem("stored")

        block = ctx.enter_context(nc.Block())

        STG = {"mla": (7, 4), "xa0": (3, 4), "dsa": (4, 4), "xa1": (3, 4), "fox": (6, 2)}
        STAGE_N = {}
        n = 0
        for name, (per, groups) in STG.items():
            STAGE_N[name] = n
            n += per * groups

        POOL_DONE = [sum(2 * (j + 1) + 2 for j in range(g + 1)) for g in range(4)]
        REL_N = 12 + 3 + 6 + 3
        AXX = mybir.AxisListType.X
        PBUF = {"mla": PB_M, "xa0": PB_X, "xa1": PB_X, "dsa": PB_D, "fox": PB_F}
        PTB = {"mla": PT_M, "xa0": PT_X, "xa1": PT_X, "dsa": PT_D, "fox": PT_F}

        def f32(ap):
            return ap.bitcast(F32)

        def chunks(w, rows=P):
            return w.rearrange("(c p) n -> p c n", p=rows)

        def wide(w, c0):
            wv = chunks(w)

            def unit(i, raw):
                r = raw.rearrange("p (c n) -> p c n", n=256)
                cols = bass.ds(i * 256 + c0, 256)
                return [(r[:, 0:4], wv[:, 0:4, cols]), (r[:, 4:8], wv[:, 4:8, cols])]
            return unit

        def narrow(w, c0, n):
            wv = chunks(w)

            def unit(i, raw):
                r = raw[:, 0:DC * n].rearrange("p (c n) -> p c n", n=n)
                return [(r[:, 0:4], wv[:, 0:4, c0:c0 + n]), (r[:, 4:8], wv[:, 4:8, c0:c0 + n])]
            return unit

        def gated(w):
            wv = chunks(w)

            def unit(i, raw):
                r = raw.rearrange("p (c n) -> p c n", n=256)
                return [(r[:, :, 0:P], wv[:, :, bass.ds(i * P, P)]),
                        (r[:, :, P:256], wv[:, :, bass.ds(i * P + FF, P)])]
            return unit

        def rows(w):
            wv = chunks(w)

            def unit(i, raw):
                r = raw.rearrange("p (c n) -> p c n", n=D)
                return [(r[:, j:j + 1], wv[:, bass.ds(i * 2 + j, 1), :]) for j in range(2)]
            return unit

        def uq(i, raw):
            r = raw[:, 0:4 * 384].rearrange("p (c n) -> p c n", n=384)
            wv = chunks(A["mla_w_uq"][0])
            w4 = wv[:, :, i * 384:i * 384 + 384].rearrange("p c (h e) -> p c h e", e=NOPE + ROPE)
            parts = []
            for c in range(4):
                parts.append((r[:, c, 0:256].rearrange("p (h e) -> p h e", e=NOPE), w4[:, c, :, 0:NOPE]))
                parts.append((r[:, c, 256:384].rearrange("p (h e) -> p h e", e=ROPE), w4[:, c, :, NOPE:]))
            return parts

        def ukv(i, raw):
            r = raw.rearrange("p (c n) -> p c n", n=D)
            wv = chunks(A["mla_w_ukv"][0])
            parts = []
            for c in range(2):
                w3 = wv[:, c, i * D:i * D + D].rearrange("p (h e) -> p h e", e=128)
                for j in range(2):
                    parts.append((r[:, c, 512 * j:512 * j + 512].rearrange("p (h e) -> p h e", e=64),
                                  w3[:, :, 64 * j:64 * j + 64]))
            return parts

        def pool_w(i, raw):
            r = raw[:, 0:512].rearrange("p (g n) -> p g n", n=P)
            wv = A["pool_w_2"][0].rearrange("g c d -> c g d")
            return [(r[:, 0:2], wv[:, 0:2]), (r[:, 2:4], wv[:, 2:4])]

        dsa_w, fox_w = A["dsa_w_in"][0], A["w_in_2"][0]
        SOURCES = {
            "mla_uq": uq, "mla_ukv": ukv, "mla_o": wide(A["mla_w_o"][0], 0),
            "dsa_q": wide(dsa_w, 0), "dsa_k": narrow(dsa_w, 1024, 256), "dsa_v": narrow(dsa_w, 1280, 256),
            "dsa_qi": wide(dsa_w, 1536), "dsa_ki": narrow(dsa_w, 2048, 72), "dsa_o": wide(A["dsa_w_o"][0], 0),
            "mod": wide(A["mod_w_2"][0], 0),
            "fox_qk": wide(fox_w, 0), "fox_v": wide(fox_w, 1024), "fox_f": narrow(fox_w, 1536, P),
            "fox_u": wide(fox_w, 1544), "fox_pool": pool_w, "fox_o": wide(A["w_out_2"][0], 0),
            "ffn_in2": gated(A["ffn_up_2"][0]), "ffn_down2": rows(A["ffn_down_2"][0]),
        }
        for layer in range(DEPTH):
            SOURCES[f"xa_kv{layer}"] = wide(A["xa_w_kv"][layer], 0)
            SOURCES[f"xa_q{layer}"] = wide(A["xa_w_q"][layer], 0)
            SOURCES[f"xa_o{layer}"] = wide(A["xa_w_o"][layer], 0)
            SOURCES[f"ffn_in{layer}"] = gated(A["ffn_w_in"][layer])
            SOURCES[f"ffn_down{layer}"] = rows(A["ffn_w_down"][layer])

        @block.sync
        def _(sp):
            sp.dma_start(KC[:, :], consts[:, 0:K_N]).then_inc(small_in, 16)
            sp.dma_start(KROT[:, :, :], consts[:, K_REP:K_ALL].rearrange("p (k n) -> p k n", n=P)).then_inc(small_in, 16)
            sp.dma_start(XN[:, :, :], A["x"][0].rearrange("(b p) d -> p b d", p=P)).then_inc(x_in, 16)

            def load(name, i, j):
                u0 = UNIT0[name]
                slot = (u0 + j) % 2
                src = SOURCES[name] if name in SOURCES else None
                if not (isinstance(i, int) and u0 + i < 2):
                    sp.wait_ge(w_split, i + (u0 - 1))
                parts = src(i, RAW[:, slot, :])
                for dst, part in parts:
                    sp.dma_start(dst, part).then_inc(w_loaded[slot], 16)

            mla_in = A["mla_w_in"][0]
            first = wide(mla_in, 0)
            last = narrow(mla_in, QRANK + KVRANK + ROPE - P, P)
            SOURCES["mla_in"] = lambda i, raw: first(i, raw) if i < 3 else last(i, raw)
            for name, nu, _ in STAGES:
                if nu > 4:
                    with sp.Fori(0, nu // 2) as pair:
                        for j in range(2):
                            load(name, pair * 2 + j, j)
                    if nu % 2:
                        load(name, nu - 1, nu - 1)
                else:
                    for i in range(nu):
                        load(name, i, i)
            sp.wait_ge(out_ready, 8)
            sp.dma_start(out[0].rearrange("(b p) d -> p b d", p=P), ON[:, :, :]).then_inc(stored, 16)
            sp.wait_ge(stored, 16)

        def by_pairs(eng, nu, body):
            if nu > 2:
                with eng.Fori(0, nu // 2) as pair:
                    for j in range(2):
                        body(pair * 2 + j, j)
            else:
                for i in range(nu // 2 * 2):
                    body(i, i)
            if nu % 2:
                body(nu - 1, 0)

        def split_hi(act, u, par, wait):
            act.wait_ge(w_loaded[par], wait[2])
            if wait[0] is not None:
                act.wait_ge(wait[0], wait[1])
            nc.scalar.activation(WH[:, par, :], RAW[:, par, :], ACT.Copy).then_inc(w_hi, 1)

        def split_lo(dve, u, par):
            dve.wait_ge(w_hi, u + 1)
            nc.vector.tensor_tensor(WL[:, par, :], RAW[:, par, :], f32(WH[:, par, :]),
                                    ALU.subtract).then_inc(w_split, 1)

        def next_hi(act, name, i, j, used, count):
            u = UNIT0[name] + 2
            if isinstance(i, int) and u + i >= N_UNITS:
                return
            par = (UNIT0[name] + j) % 2
            loads = LOADED[u + i] if isinstance(i, int) else (i - j) * 16 + LOADED[u + j]
            split_hi(act, u + i, par, (used, count, loads))

        def next_lo(dve, name, i, j):
            u = UNIT0[name] + 2
            if isinstance(i, int) and u + i >= N_UNITS:
                return
            split_lo(dve, u + i, (UNIT0[name] + j) % 2)

        @block.tensor
        def _(pe):
            for s, v in ((tile_ready, 4), (logits_ready, 4), (turned, 4), (av_done, 4), (step_used, 8)):
                pe.sem_inc(s, v)

            def three(out_ap, pairs_w, pairs_x, weights_first=True):
                n = 3 * len(pairs_w)
                i = 0
                for (wh, wl), (xh, xl) in zip(pairs_w, pairs_x):
                    for a, b in ((wh, xh), (wh, xl), (wl, xh)):
                        l, r = (a, b) if weights_first else (b, a)
                        mm = nc.tensor.matmul(out_ap, l, r, start=(i == 0), stop=(i == n - 1))
                        i += 1
                return mm

            def tile_start(t):
                pe.wait_ge(tile_free, t - 3)

            def wcols(slot, n, k0, k1, nch=DC):
                return [(WH[:, slot, c * n + k0:c * n + k1], WL[:, slot, c * n + k0:c * n + k1]) for c in range(nch)]

            def xpairs(hi=XH, lo=XL, nch=DC, c0=0):
                return [(hi[:, c0 + c, :], lo[:, c0 + c, :]) for c in range(nch)]

            def wait_unit(name, i):
                pe.wait_ge(w_split, i + (UNIT0[name] + 1))

            def wide_stage(name, xs, n=S):
                def unit(i, j):
                    wait_unit(name, i)
                    slot = (UNIT0[name] + j) % 2
                    for k in range(2):
                        b = (TILE0[name] + 2 * j + k) % 4
                        tile_start(i * 2 + (TILE0[name] + k))
                        three(bank[b][:, 0:n], wcols(slot, 256, P * k, P * k + P), xs).then_inc(tile_ready, 1)
                by_pairs(pe, UNITS[name], unit)

            def fill_ready(name):
                pe.wait_ge(x_split, FILL0[name] + 8)

            def norm_sums(name, rows_ready, sq_bank, mean_bank=None):
                k = NORM_I[name]
                if mean_bank is not None:
                    for c in range(DC):
                        pe.wait_ge(*rows_ready(c))
                        mm = nc.tensor.matmul(mean_bank[:, :], ONES, ZB[:, c, :], start=(c == 0), stop=(c == DC - 1))
                    mm.then_inc(mean_ready, 1)
                for c in range(DC):
                    pe.wait_ge(squared, 8 * k + c + 1)
                    nc.tensor.matmul(sq_bank[:, :], ONES, SQ[:, c % 4, :], start=(c == 0),
                                     stop=(c == DC - 1)).then_inc(sq_summed, 1)

            def proj_norm(stage, norm):
                norm_sums(norm, lambda c: (tile_free, TILE0[stage] + c + 1), bank[7], bank[6])

            def attention(name, groups, heads, logits, av, o_free, n_logit_stage):
                steps = 4 * heads
                per = STG[name][0]

                def group(g):
                    s0 = STEP0[name]

                    def do_logits(i):
                        if i == 0:
                            pe.wait_ge(staged, g * per + (STAGE_N[name] + n_logit_stage))
                        pe.wait_ge(max_done, g * steps + (s0 + i - 3))
                        logits(g, i, bank[i % 4]).then_inc(logits_ready, 1)

                    def do_turn(i):
                        qb = i % 4
                        pe.wait_ge(probs_ready, g * steps + (s0 + i + 1))
                        pe.wait_ge(pt_done, g * steps + (s0 + i - 1))
                        pb = PBUF[name]
                        nkb = 2 if name[:2] == "xa" else qb + 1
                        for kb in range(nkb):
                            mm = nc.tensor.transpose(bank[4 + i % 2][:, P * kb:P * kb + P],
                                                     pb[:, i % 4, P * kb:P * kb + P], IDN)
                        mm.then_inc(turned, 1)

                    def do_av(i):
                        if i == 0:
                            pe.wait_ge(staged, g * per + (STAGE_N[name] + per))
                        pe.wait_ge(pt_done, g * steps + (s0 + i + 1))
                        o_free(pe, g, i)
                        av(g, i).then_inc(av_done, 1)

                    for i in range(3):
                        do_logits(i)
                    for i in range(steps):
                        do_turn(i)
                        if i + 3 < steps:
                            do_logits(i + 3)
                        if i >= 2:
                            do_av(i - 2)
                    do_av(steps - 2)
                    do_av(steps - 1)

                with pe.Fori(0, groups) as g:
                    group(g)


            def head_av(name, v):
                def av(g, i):
                    hh, qb = divmod(i, 4)
                    o = bank[6 + hh // 2][64 * (hh % 2):64 * (hh % 2) + 64, P * qb:P * qb + P]
                    for kb in range(qb + 1):
                        mm = nc.tensor.matmul(o, v(hh, kb), PTB[name][:, i % 2, P * kb:P * kb + P],
                                              start=(kb == 0), stop=(kb == qb))
                    return mm
                return av

            pe.wait_ge(small_in, 32)
            pe.wait_ge(x_in, 16)
            for c in range(8):
                t = TILE0["x_in"] + c
                tile_start(t)
                for b in range(NQ):
                    mm = nc.tensor.transpose(bank[t % 4][:, P * b:P * b + P], XN[:, b, P * c:P * c + P], IDN)
                mm.then_inc(tile_ready, 1)
            pe.wait_ge(rows_in, 16 * 14)
            for k in range(4):
                mm = nc.tensor.transpose(bank[7][:, P * k:P * k + P], VR[:, k, :], IDN)
            mm.then_inc(cols_t, 1)

            fill_ready("x0")
            for i in range(4):
                wait_unit("mla_in", i)
                slot = (UNIT0["mla_in"] + i) % 2
                for k in range(2 if i < 3 else 1):
                    t = TILE0["mla_in"] + 2 * i + k
                    tile_start(t)
                    w = wcols(slot, 256 if i < 3 else P, P * k, P * k + P)
                    three(bank[t % 4][:, :], w, xpairs()).then_inc(tile_ready, 1)
            for c in range(6):
                pe.wait_ge(c_affine, c + 1)
                q = c < 4
                mm = nc.tensor.matmul(bank[6 if q else 7][:, :], ONES, MSQ[:, c % 4, :], start=c in (0, 4), stop=c in (3, 5))
                mm.then_inc(rope_mm, 1)
            for i in range(4):
                wait_unit("mla_uq", i)
                slot = (UNIT0["mla_uq"] + i) % 2
                if i == 0:
                    pe.wait_ge(c_split, 4)
                for k in range(3):
                    t = TILE0["mla_uq"] + 3 * i + k
                    tile_start(t)
                    three(bank[t % 4][:, :], wcols(slot, 384, P * k, P * k + P, 4), xpairs(CH, CL, 4)).then_inc(tile_ready, 1)
            for r in range(5):
                if r == 0:
                    pe.wait_ge(tile_free, TILE0["mla_in"] + 7)
                else:
                    pe.wait_ge(tile_free, TILE0["mla_uq"] + 3 * r)
                if r >= 2:
                    pe.wait_ge(rope_dve, 3 * (r - 2) + 2)
                if r == 0:
                    nc.tensor.matmul(bank[6][:, :], REP, KRAW[:, :], start=True, stop=True)
                    mm = nc.tensor.matmul(bank[4][:, :], ROT, KRAW[:, :], start=True, stop=True)
                else:
                    mm = nc.tensor.matmul(bank[4 + r % 2][:, :], PERM, QR[:, r - 1, :], start=True, stop=True)
                mm.then_inc(rope_mm, 1)
            for i in range(2):
                wait_unit("mla_ukv", i)
                slot = (UNIT0["mla_ukv"] + i) % 2
                if i == 0:
                    pe.wait_ge(c_split, 6)
                for k in range(8):
                    t = TILE0["mla_ukv"] + 8 * i + k
                    tile_start(t)
                    if k < 4:
                        mm = three(bank[t % 4][:, :], wcols(slot, D, P * k, P * k + P, 2), xpairs(CH, CL, 2, 4))
                    else:
                        w = wcols(slot, D, 512, D, 2)
                        x = [(CH[:, 4 + c, P * (k - 4):P * (k - 3)], CL[:, 4 + c, P * (k - 4):P * (k - 3)]) for c in range(2)]
                        mm = three(bank[t % 4][:, :], w, x, weights_first=False)
                    mm.then_inc(tile_ready, 1)
            pe.wait_ge(tile_free, TILE0["mla_o"])
            pe.wait_ge(rope_dve, 15)

            def mla_logits(g, i, b):
                hh, qb = divmod(i, 4)
                w = P * qb + P
                lo, hi = 64 * (hh % 2), 64 * (hh % 2) + 64
                nc.tensor.matmul(b[:, 0:w], Q_M[lo:hi, hh // 2, P * qb:P * qb + P], K_M[lo:hi, hh // 2, 0:w],
                                 start=True, stop=False)
                return nc.tensor.matmul(b[:, 0:w], Q_M[32 * hh:32 * hh + 32, 2, P * qb:P * qb + P],
                                        KR[32 * hh:32 * hh + 32, 0:w], start=False, stop=True)

            def o_split(fill):
                def o_free(pe, g, i):
                    if i in (0, 8):
                        pe.wait_ge(x_split, g * 2 + (FILL0[fill] + i // 8 - 1))
                return o_free

            attention("mla", 4, 4, mla_logits, head_av("mla", lambda hh, kb: V_M[:, kb, 64 * hh:64 * hh + 64]),
                      o_split("mla_o"), 5)
            fill_ready("mla_o")
            wide_stage("mla_o", xpairs())
            proj_norm("mla_o", "ln0")

            def cross_attention(layer):
                pe.wait_ge(mem_in, 16 * (layer + 1))
                for c in range(DC):
                    t = TILE0[f"mem{layer}"] + c
                    tile_start(t)
                    for b in range(2):
                        mm = nc.tensor.transpose(bank[t % 4][:, P * b:P * b + P], MN[:, b, P * c:P * c + P], IDN)
                    mm.then_inc(tile_ready, 1)
                pe.wait_ge(tile_free, TILE0[f"xa_kv{layer}"])
                name = f"xa_kv{layer}"

                def unit(first):
                    def one(i, j):
                        v = i + first
                        wait_unit(name, v)
                        slot = (UNIT0[name] + j) % 2
                        for k in range(2):
                            b = (TILE0[name] + 2 * j + k) % 4
                            tile_start(v * 2 + (TILE0[name] + k))
                            if first == 0:
                                x = [(MH[:, c, :], ML[:, c, :]) for c in range(DC)]
                                mm = three(bank[b][:, 0:MEM], wcols(slot, 256, P * k, P * k + P), x)
                            else:
                                x = [(MH[:, c, P * k:P * k + P], ML[:, c, P * k:P * k + P]) for c in range(DC)]
                                mm = three(bank[b][:, 0:MEM], wcols(slot, 256, 0, 256), x, weights_first=False)
                            mm.then_inc(tile_ready, 1)
                    return one
                by_pairs(pe, 4, unit(0))
                by_pairs(pe, 4, unit(4))
                fill_ready(f"ln{3 * layer}")
                wide_stage(f"xa_q{layer}", xpairs())
                pe.wait_ge(tile_free, TILE0[f"xa_o{layer}"])

                def logits(g, i, b):
                    for c in range(2):
                        mm = nc.tensor.matmul(b[:, 0:MEM], Q_X[:, c, P * i:P * i + P],
                                              KX[:, bass.ds(g * 2 + c, 1), :], start=(c == 0), stop=(c == 1))
                    return mm

                def av(g, i):
                    for d in range(2):
                        for kb in range(2):
                            mm = nc.tensor.matmul(bank[6 + d][:, P * i:P * i + P], V_X[:, kb, P * d:P * d + P],
                                                  PT_X[:, i % 2, P * kb:P * kb + P], start=(kb == 0), stop=(kb == 1))
                    return mm

                def o_free(pe, g, i):
                    if i == 0:
                        pe.wait_ge(x_split, g * 2 + FILL0[f"xa{layer}_o"])
                attention(f"xa{layer}", 4, 1, logits, av, o_free, 2)
                fill_ready(f"xa{layer}_o")
                wide_stage(f"xa_o{layer}", xpairs())
                proj_norm(f"xa_o{layer}", f"ln{3 * layer + 1}")

            def down_stage(f):
                name = f"ffn_down{f}"

                def unit(i, j, first, last):
                    wait_unit(name, i)
                    pe.wait_ge(hid_split, i * 2 + (FC * f + 2))
                    slot = (UNIT0[name] + j) % 2
                    for n in range(DC):
                        for c in range(2):
                            x = i * 2 + c
                            w = [h[:, slot, D * c + P * n:D * c + P * n + P] for h in (WH, WL)]
                            hh, hl = HH[:, bass.ds(x, 1), :], HL[:, bass.ds(x, 1), :]
                            for k, (a, b) in enumerate(((w[0], hh), (w[0], hl), (w[1], hh))):
                                mm = nc.tensor.matmul(bank[n][:, :], a, b, start=(first and c == 0 and k == 0),
                                                      stop=(last and c == 1 and k == 2))
                        if last:
                            mm.then_inc(y_ready, 1)
                    if not last:
                        mm.then_inc(unit_used, 1)
                unit(0, 0, True, False)
                with pe.Fori(0, 4) as pair:
                    for j in range(2):
                        unit(pair * 2 + (1 + j), 1 + j, False, False)
                unit(9, 9, False, False)
                unit(10, 10, False, True)

            def feed_forward(f, fill, norm):
                fill_ready(fill)
                wide_stage(f"ffn_in{f}", xpairs())
                pe.wait_ge(tile_free, TILE0[f"ffn_in{f}"] + 2 * FC)
                down_stage(f)
                if norm[0] == "l":
                    norm_sums(norm, lambda c: (y_free, DC * f + c + 1), bank[1], bank[0])

            cross_attention(0)
            feed_forward(0, "ln1", "ln2")

            fill_ready("ln2")
            wide_stage("dsa_q", xpairs())
            wait_unit("dsa_k", 0)
            slot = UNIT0["dsa_k"] % 2
            for k in range(2):
                t = TILE0["dsa_k"] + k
                tile_start(t)
                three(bank[t % 4][:, :], wcols(slot, 256, P * k, P * k + P), xpairs()).then_inc(tile_ready, 1)
            for k in range(4):
                t = TILE0["dsa_k"] + 2 + k
                tile_start(t)
                pe.wait_ge(tile_free, TILE0["dsa_k"] + k // 2 + 1)
                nc.tensor.matmul(bank[t % 4][:, :], SEL[k % 2], RL[:, k // 2, :], start=True, stop=True).then_inc(tile_ready, 1)

            def row_tiles(name, n0, tiles0, cols, n):
                for k in range(NQ):
                    t = tiles0 + k
                    tile_start(t)
                    x = [(XH[:, c, P * k:P * k + P], XL[:, c, P * k:P * k + P]) for c in range(DC)]
                    three(bank[t % 4][:, 0:n], cols, x, weights_first=False).then_inc(tile_ready, 1)

            wait_unit("dsa_v", 0)
            row_tiles("dsa_v", 0, TILE0["dsa_v"], wcols(UNIT0["dsa_v"] % 2, 256, 0, 256), 256)
            wide_stage("dsa_qi", xpairs())
            wait_unit("dsa_ki", 0)
            slot = UNIT0["dsa_ki"] % 2
            t = TILE0["dsa_ki"]
            tile_start(t)
            three(bank[t % 4][0:72, :], wcols(slot, 72, 0, 72), xpairs()).then_inc(tile_ready, 1)
            row_tiles("dsa_ki", 0, t + 1, wcols(slot, 72, 64, 72), 8)
            tile_start(t + 5)
            pe.wait_ge(tile_free, t + 1)
            nc.tensor.matmul(bank[(t + 5) % 4][:, :], SEL[0][0:64, :], RL[0:64, 0, :], start=True,
                             stop=True).then_inc(tile_ready, 1)
            pe.wait_ge(tile_free, TILE0["dsa_ki"] + 6)
            for i in range(NQ * IDXH):
                qb, h = divmod(i, IDXH)
                if i >= 4:
                    pe.wait_ge(idx_relu, i - 3)
                w = P * qb + P
                lo = 64 * (h % 2)
                nc.tensor.matmul(bank[4 + i % 4][:, 0:w], QI[lo:lo + 64, h // 2, P * qb:P * qb + P], KI[lo:lo + 64, 0:w],
                                 start=True, stop=True).then_inc(idx_ready, 1)
            pe.wait_ge(rel_dve, REL_N)
            pe.wait_ge(idx_relu, NQ * IDXH)
            done = 4
            for kb in range(NQ):
                n = NQ - kb
                with pe.Fori(0, 4) as kg:
                    pe.wait_ge(bias_free, kg * n + done)
                    for k in range(32):
                        pe.wait_ge(step_done, kg * 32 + (P * kb + k + 1))
                        for qb in range(kb, NQ):
                            mm = nc.tensor.matmul(bank[qb][:, 16 * k:16 * k + 16],
                                                  ST[:, k % 8, P * qb:P * qb + P], DEL[:, :], start=(k == 0), stop=(k == 31),
                                                  skip_group_check=True)
                        mm.then_inc(step_used, 1)
                done += 4 * n

            def dsa_logits(g, i, b):
                hh, qb = divmod(i, 4)
                w = P * qb + P
                lo = 64 * (hh % 2)
                return nc.tensor.matmul(b[:, 0:w], Q_D[lo:lo + 64, hh // 2, P * qb:P * qb + P], K_D[lo:lo + 64, 0:w],
                                        start=True, stop=True)

            def dsa_o_free(pe, g, i):
                if i in (0, 8):
                    pe.wait_ge(o_copied, g * 2 + (i // 8 + 1))
            pe.wait_ge(bias_free, done)
            attention("dsa", 4, 4, dsa_logits, head_av("dsa", lambda hh, kb: V_D[:, kb, :]), dsa_o_free, 3)
            fill_ready("dsa_o")
            wide_stage("dsa_o", xpairs())
            proj_norm("dsa_o", "ln3")
            cross_attention(1)
            feed_forward(1, "ln4", "ln5")

            pe.wait_ge(affine, 8 * NORM_I["ln5"] + 8)
            pe.wait_ge(mod_hi, 2)
            name = "mod"

            def mod_unit(i, j):
                wait_unit(name, i)
                slot = (UNIT0[name] + j) % 2
                t = i + TILE0[name]
                tile_start(t)
                x = [tuple(h[:, c:c + 1].broadcast_to((P, P)) for h in (CAH, CAL)) for c in range(DC)]
                three(bank[(TILE0[name] + j) % 4][:, 0:256], wcols(slot, 256, 0, 256), x,
                      weights_first=False).then_inc(tile_ready, 1)
            with pe.Fori(0, 6) as four:
                for j in range(4):
                    mod_unit(four * 4 + j, j)
            norm_sums("rms1", None, bank[7])
            fill_ready("rms1")
            wide_stage("fox_qk", xpairs())
            for i in range(2):
                wait_unit("fox_v", i)
                row_tiles("fox_v", 0, TILE0["fox_v"] + 4 * i, wcols((UNIT0["fox_v"] + i) % 2, 256, 0, 256), 256)
            wait_unit("fox_f", 0)
            slot = UNIT0["fox_f"] % 2
            t = TILE0["fox_f"]
            tile_start(t)
            three(bank[t % 4][:, :], wcols(slot, P, 0, P), xpairs()).then_inc(tile_ready, 1)
            for i in range(2):
                wait_unit("fox_u", i)
                slot = (UNIT0["fox_u"] + i) % 2
                for k in range(2):
                    t = TILE0["fox_u"] + 2 * i + k
                    tile_start(t)
                    three(bank[t % 4][:, :], wcols(slot, 256, P * k, P * k + P), xpairs()).then_inc(tile_ready, 1)
            pe.wait_ge(f_dve, 4)
            for b in range(NQ):
                mm = nc.tensor.transpose(bank[7][:, P * b:P * b + P], FG[:, 3, P * b:P * b + P], IDN)
            mm.then_inc(f_mm, 1)
            for h in range(FOXH):
                if h >= 2:
                    pe.wait_ge(f_act, 3 + h - 1)
                nc.tensor.matmul(bank[5 + h % 2][:, :], KC[0:FOXH, K_ID + h:K_ID + h + 1].broadcast_to((FOXH, P)),
                                 FG[0:FOXH, 3, :], start=True, stop=True).then_inc(f_mm, 1)
            wait_unit("fox_pool", 0)
            slot = UNIT0["fox_pool"] % 2
            for g in range(4):
                t = TILE0["fox_pool"] + g
                tile_start(t)
                pe.wait_ge(pool_split, g + 1)
                three(bank[t % 4][:, :], [(WH[:, slot, P * g:P * g + P], WL[:, slot, P * g:P * g + P])],
                      [(PLH[:, g, :], PLL[:, g, :])]).then_inc(tile_ready, 1)
            pe.wait_ge(tile_free, TILE0["fox_o"])
            pe.wait_ge(f_act, 11)

            def fox_logits(g, i, b):
                hh, qb = divmod(i, 4)
                w = P * qb + P
                lo, hi = 64 * (hh % 2), 64 * (hh % 2) + 64
                return nc.tensor.matmul(b[:, 0:w], Q_F[lo:hi, hh // 2, P * qb:P * qb + P], K_F[lo:hi, hh // 2, 0:w],
                                        start=True, stop=True)

            def fox_o_free(pe, g, i):
                if i in (0, 8):
                    pe.wait_ge(x_split, g * 2 + (FILL0["fox_o"] + 4 + i // 8 - 1))
            attention("fox", 2, 4, fox_logits, head_av("fox", lambda hh, kb: V_F[:, kb, 64 * hh:64 * hh + 64]),
                      fox_o_free, 4)
            fill_ready("fox_o")
            wide_stage("fox_o", xpairs())
            norm_sums("rms2", None, bank[7])
            feed_forward(2, "rms2", "rms3")
            pe.wait_ge(y_free, DC * 2 + DC)
            norm_sums("rms3", None, bank[1])
            for b in range(NQ):
                for half in range(2):
                    n = 2 * b + half
                    if b == 0:
                        pe.wait_ge(affine, 8 * NORM_I["rms3"] + 4 * half + 4)
                    if n >= 4:
                        pe.wait_ge(out_ready, n - 3)
                    for k in range(4):
                        mm = nc.tensor.transpose(bank[4 + n % 4][:, P * k:P * k + P],
                                                 ZB[:, 4 * half + k, P * b:P * b + P], IDN)
                    mm.then_inc(f_mm, 1)

        @block.scalar
        def _(act):
            for s in (exp_done, pt_done, tile_free):
                act.sem_inc(s, 4)

            def copy(dst, src, **kw):
                return nc.scalar.activation(dst, src, ACT.Copy, **kw)

            for u in range(2):
                split_hi(act, u, u, (None, 0, LOADED[u]))
            for c in range(8):
                t = TILE0["x_in"] + c
                act.wait_ge(tile_ready, t + 1)
                copy(XT[:, c, :], bank[t % 4][:, :])
                copy(XH[:, c, :], bank[t % 4][:, :]).then_inc(tile_free, 1)
            act.wait_ge(cols_t, 1)
            copy(COL[:, :], bank[7][:, :]).then_inc(cols_done, 1)
            act.wait_ge(cols_done, 2)
            nc.scalar.activation(CA[:, :], COL[:, COLS["c"]:COLS["c"] + 8], ACT.Silu).then_inc(mod_hi, 1)
            act.wait_ge(mod_hi, 1)
            copy(CAH[:, :], CA[:, :]).then_inc(c_hi, 1)
            act.wait_ge(trig, 6)
            nc.scalar.activation(SIN[:, :], RT[:, 0, :], ACT.Sin)
            nc.scalar.activation(COS[:, :], RT[:, 1, :], ACT.Sin).then_inc(trig_act, 1)

            def after_unit(name, i, j, tiles_through):
                next_hi(act, name, i, j, tile_ready, tiles_through)

            for i in range(4):
                for k in range(2 if i < 3 else 1):
                    t = TILE0["mla_in"] + 2 * i + k
                    act.wait_ge(tile_ready, t + 1)
                    dst = CR[:, 2 * i + k, :] if i < 3 else KRAW[:, :]
                    copy(dst, bank[t % 4][:, :]).then_inc(tile_free, 1)
                after_unit("mla_in", i, i, TILE0["mla_in"] + min(2 * i + 2, 7))
            for c in range(6):
                if c >= 4:
                    act.wait_ge(rope_mm, c - 3)
                act.wait_ge(tile_free, TILE0["mla_in"] + c + 1)
                nc.scalar.activation(MSQ[:, c % 4, :], CR[:, c, :], ACT.Square).then_inc(c_affine, 1)
            act.wait_ge(eps_done, 4)
            for q in range(2):
                act.wait_ge(rope_mm, 4 if q == 0 else 6)
                nc.scalar.activation(RQ[:, q, :], bank[6 + q][:, :], ACT.Sqrt, bias=EPS[:, 1:2],
                                     scale=float(D // (QRANK if q == 0 else KVRANK))).then_inc(std_done, 1)
            for c in range(6):
                act.wait_ge(c_scaled, 3 + c)
                g = COLS["q_norm"] + c
                nc.scalar.activation(CR[:, c, :], CR[:, c, :], ACT.Copy, scale=COL[:, g:g + 1]).then_inc(c_affine, 1)
                act.wait_ge(c_affine, 6 + 2 * c + 1)
                copy(CH[:, c, :], CR[:, c, :]).then_inc(c_affine, 1)
            for i in range(4):
                for k in range(3):
                    t = TILE0["mla_uq"] + 3 * i + k
                    act.wait_ge(tile_ready, t + 1)
                    dst = QN[:, 2 * i + k, :] if k < 2 else QR[:, i, :]
                    copy(dst, bank[t % 4][:, :]).then_inc(tile_free, 1)
                after_unit("mla_uq", i, i, TILE0["mla_uq"] + 3 * i + 3)
            for i in range(2):
                for k in range(8):
                    t = TILE0["mla_ukv"] + 8 * i + k
                    act.wait_ge(tile_ready, t + 1)
                    dst = KN[:, 4 * i + k, :] if k < 4 else VM[:, k - 4, 512 * i:512 * i + 512]
                    copy(dst, bank[t % 4][:, :]).then_inc(tile_free, 1)
                after_unit("mla_ukv", i, i, TILE0["mla_ukv"] + 8 * i + 8)


            def attention(name, groups, heads, scale, out_tile):
                steps = 4 * heads
                s0 = STEP0[name]
                xa = name[:2] == "xa"
                with act.Fori(0, groups) as g:
                    def exps(i):
                        w = MEM if xa else P * (i % 4) + P
                        act.wait_ge(negmax_done, g * steps + (s0 + i + 1))
                        pb = PBUF[name][:, i % 4, 0:w]
                        nc.scalar.activation(pb, pb, ACT.Exp, bias=NM[:, i % 4:i % 4 + 1], scale=scale,
                                             accum_out=RS[:, i % 4:i % 4 + 1]).then_inc(exp_done, 1)

                    def evac(i):
                        w = MEM if xa else P * (i % 4) + P
                        act.wait_ge(turned, g * steps + (s0 + i + 1))
                        act.wait_ge(av_done, g * steps + (s0 + i - 1))
                        copy(PTB[name][:, i % 2, 0:w], bank[4 + i % 2][:, 0:w]).then_inc(pt_done, 1)

                    def outs(i):
                        if xa:
                            if i == 3:
                                act.wait_ge(av_done, g * steps + (s0 + 4))
                                for d in range(2):
                                    out_tile(g, d)
                        elif i % 8 == 7:
                            act.wait_ge(av_done, g * steps + (s0 + i + 1))
                            out_tile(g, i // 8)
                    for i in range(steps):
                        exps(i)
                        if i >= 2:
                            evac(i - 2)
                        if i >= 5:
                            outs(i - 5)
                    evac(steps - 2)
                    evac(steps - 1)
                    for i in range(max(0, steps - 5), steps):
                        outs(i)

            def o_hi(fill, c0=0):
                def out_tile(g, k):
                    copy(XH[:, bass.ds(g * 2 + (k + c0), 1), :], bank[6 + k][:, :]).then_inc(x_hi, 1)
                return out_tile

            attention("mla", 4, 4, MLA_SCALE, o_hi("mla_o"))

            def wide_units(name, per_unit, pairs=None):
                def unit(i, j):
                    per_unit(i, j)
                    after_unit(name, i, j, i * 2 + (TILE0[name] + 2))
                by_pairs(act, UNITS[name], unit)

            def nothing(i, j):
                pass

            def norm(name, ready, var_bank, g_col, b_col, out_to_x, hi, src):
                k = NORM_I[name]
                for c in range(DC):
                    act.wait_ge(*ready(c))
                    if 8 * k + c >= 4:
                        act.wait_ge(sq_summed, 8 * k + c - 3)
                    nc.scalar.activation(SQ[:, c % 4, :], src[:, c, :], ACT.Square).then_inc(squared, 1)
                act.wait_ge(sq_summed, 8 * k + 8)
                nc.scalar.activation(STD[:, :], var_bank[:, :], ACT.Sqrt,
                                     bias=EPS[:, 0:1] if src is ZB else EPS[:, 1:2]).then_inc(std_done, 1)
                dst = XT if out_to_x else ZB
                for c in range(DC):
                    act.wait_ge(scaled, 8 * k + c + 1)
                    gain = g_col(c)
                    if b_col is None:
                        nc.scalar.activation(dst[:, c, :], ZB[:, c, :], ACT.Copy, scale=gain).then_inc(affine, 1)
                    else:
                        nc.scalar.activation(dst[:, c, :], ZB[:, c, :], ACT.Identity, scale=gain,
                                             bias=b_col(c)).then_inc(affine, 1)
                    if hi:
                        act.wait_ge(affine, 8 * k + c + 1)
                        copy(XH[:, c, :], dst[:, c, :]).then_inc(x_hi, 1)

            def ln(idx, var_bank, hi=True):
                def col(what):
                    return lambda c: COL[:, COLS[what] + 8 * idx + c:COLS[what] + 8 * idx + c + 1]
                norm(f"ln{idx}", lambda c: (centred, 8 * idx + c + 1), var_bank, col("ln_g"), col("ln_b"), True, hi, ZB)

            wide_units("mla_o", nothing)
            ln(0, bank[7])

            def cross_attention(layer):
                for c in range(DC):
                    t = TILE0[f"mem{layer}"] + c
                    act.wait_ge(tile_ready, t + 1)
                    copy(MH[:, c, :], bank[t % 4][:, 0:MEM]).then_inc(mod_done, 1)
                name = f"xa_kv{layer}"

                def kv(first):
                    def unit(i, j):
                        v = i + first
                        for k in range(2):
                            t = (TILE0[name] + 2 * j + k) % 4
                            act.wait_ge(tile_ready, v * 2 + (TILE0[name] + k + 1))
                            if first == 0:
                                dst = KX[:, bass.ds(i * 2 + k, 1), :]
                            else:
                                dst = VX[:, k, bass.ds(i * 256, 256)]
                            copy(dst, bank[t][:, 0:MEM]).then_inc(tile_free, 1)
                        after_unit(name, v, j, v * 2 + (TILE0[name] + 2))
                    return unit
                by_pairs(act, 4, kv(0))
                by_pairs(act, 4, kv(4))
                q = f"xa_q{layer}"

                def queries(i, j):
                    for k in range(2):
                        act.wait_ge(tile_ready, i * 2 + (TILE0[q] + k + 1))
                        copy(QX[:, bass.ds(i * 2 + k, 1), :], bank[(TILE0[q] + 2 * j + k) % 4][:, :]).then_inc(tile_free, 1)
                wide_units(q, queries)
                attention(f"xa{layer}", 4, 1, (D // 4) ** -0.5, o_hi(f"xa{layer}_o"))
                wide_units(f"xa_o{layer}", nothing)
                ln(3 * layer + 1, bank[7])

            def hidden(f):
                name = f"ffn_in{f}"

                def unit(i, j):
                    b0, b1 = bank[(TILE0[name] + 2 * j) % 4], bank[(TILE0[name] + 2 * j + 1) % 4]
                    t = i * 2 + TILE0[name]
                    act.wait_ge(tile_ready, t + 1)
                    if f < 2:
                        nc.scalar.activation(SG[:, j, :], b0[:, :], ACT.Silu).then_inc(silu_done, 1)
                    else:
                        for n, b in enumerate((b0, b1)):
                            if n:
                                act.wait_ge(tile_ready, t + 2)
                            w2, cb = COLS["conv_w2"] + FC * n, COLS["conv_b"] + FC * n
                            nc.scalar.activation((SG, HF)[n][:, j, :], b[:, :], ACT.Identity,
                                                 scale=COL[:, bass.ds(i + w2, 1)],
                                                 bias=COL[:, bass.ds(i + cb, 1)]).then_inc(tap_done, 1)
                        act.wait_ge(conv_acc, i * 4 + 2)
                        nc.scalar.activation(SG[:, j, :], SG[:, j, :], ACT.Silu).then_inc(silu_done, 1)
                    act.wait_ge(tile_free, t + 2)
                    copy(HH[:, bass.ds(i, 1), :], HF[:, j, :]).then_inc(hid_hi, 1)
                    after_unit(name, i, j, t + 2)
                by_pairs(act, FC, unit)
                down = f"ffn_down{f}"
                u0 = 10 * f
                next_hi(act, down, 0, 0, unit_used, u0 + 1)
                with act.Fori(0, 4) as pair:
                    for j in range(2):
                        next_hi(act, down, pair * 2 + (1 + j), 1 + j, unit_used, pair * 2 + (u0 + 2 + j))
                next_hi(act, down, 9, 9, unit_used, u0 + 10)
                next_hi(act, down, 10, 10, y_ready, DC * f + 8)

            cross_attention(0)
            hidden(0)
            ln(2, bank[1])

            def dsa_q(i, j):
                for k in range(2):
                    act.wait_ge(tile_ready, i * 2 + (TILE0["dsa_q"] + k + 1))
                    copy(QD[:, bass.ds(i * 2 + k, 1), :], bank[(TILE0["dsa_q"] + 2 * j + k) % 4][:, :],
                         scale=0.125).then_inc(tile_free, 1)
            wide_units("dsa_q", dsa_q)
            for k in range(6):
                t = TILE0["dsa_k"] + k
                act.wait_ge(tile_ready, t + 1)
                copy(RL[:, k, :] if k < 2 else KD[:, k - 2, :], bank[t % 4][:, :]).then_inc(tile_free, 1)
            after_unit("dsa_k", 0, 0, TILE0["dsa_k"] + 2)
            for k in range(4):
                t = TILE0["dsa_v"] + k
                act.wait_ge(tile_ready, t + 1)
                copy(VD[:, k, :], bank[t % 4][:, 0:256]).then_inc(tile_free, 1)
            after_unit("dsa_v", 0, 0, TILE0["dsa_v"] + 4)

            def dsa_qi(i, j):
                for k in range(2):
                    t = TILE0["dsa_qi"] + 2 * i + k
                    act.wait_ge(tile_ready, t + 1)
                    copy(QI[:, 2 * i + k, :], bank[t % 4][:, :], scale=0.125).then_inc(tile_free, 1)
            wide_units("dsa_qi", dsa_qi)
            t = TILE0["dsa_ki"]
            act.wait_ge(tile_ready, t + 1)
            copy(RL[0:64, 0, :], bank[t % 4][0:64, :]).then_inc(tile_free, 1)
            for k in range(NQ):
                act.wait_ge(tile_ready, t + 2 + k)
                copy(WIX[:, k, :], bank[(t + 1 + k) % 4][:, 0:8], scale=float(IDXH ** -0.5)).then_inc(tile_free, 1)
            act.wait_ge(tile_ready, t + 6)
            copy(KI[:, :], bank[(t + 5) % 4][:, :]).then_inc(tile_free, 1)
            after_unit("dsa_ki", 0, 0, t + 6)
            for i in range(NQ * IDXH):
                qb = i // IDXH
                w = P * qb + P
                act.wait_ge(idx_ready, i + 1)
                if i >= 2:
                    act.wait_ge(idx_acc, i - 1)
                nc.scalar.activation(RL[:, i % 2, 0:w], bank[4 + i % 4][:, 0:w], ACT.Relu).then_inc(idx_relu, 1)
            copy(VK[:, :, :], VD[:, :, :]).then_inc(v_moved, 1)

            def o_copy(g, k):
                copy(QD[:, bass.ds(g * 2 + k, 1), :], bank[6 + k][:, :]).then_inc(o_copied, 1)
            act.sem_inc(o_copied, 2)
            attention("dsa", 4, 4, 1.0, o_copy)
            for c in range(DC):
                act.wait_ge(o_copied, 2 + 8)
                if c == 0:
                    act.wait_ge(av_done, STEP0["dsa"] + 64)
                copy(XH[:, c, :], QD[:, c, :]).then_inc(x_hi, 1)
            wide_units("dsa_o", nothing)
            ln(3, bank[7])
            cross_attention(1)
            hidden(1)
            ln(5, bank[1], hi=False)

            with act.Fori(0, 6) as four:
                for j in range(4):
                    i = four * 4 + j
                    u = UNIT0["mod"] + 2
                    par = (UNIT0["mod"] + j) % 2
                    loads = four * 64 + LOADED[u + j]
                    split_hi(act, i + u, par, (tile_ready, i + (TILE0["mod"] + 1), loads))

            def rms(name, ready, var_bank, gain, shift, hi):
                norm(name, ready, var_bank, lambda c: gain[:, c:c + 1],
                     None if shift is None else (lambda c: shift[:, c:c + 1]), False, hi, XT)
            rms("rms1", lambda c: (affine, 8 * NORM_I["ln5"] + c + 1), bank[7], G1, MODC[:, 0:8], True)

            def fox_qk(i, j):
                for k in range(2):
                    act.wait_ge(tile_ready, i * 2 + (TILE0["fox_qk"] + k + 1))
                    copy(QF[:, bass.ds(i * 2 + k, 1), :], bank[(TILE0["fox_qk"] + 2 * j + k) % 4][:, :]).then_inc(tile_free, 1)
            wide_units("fox_qk", fox_qk)
            for i in range(2):
                for k in range(NQ):
                    t = TILE0["fox_v"] + 4 * i + k
                    act.wait_ge(tile_ready, t + 1)
                    copy(VF[:, k, 256 * i:256 * i + 256], bank[t % 4][:, 0:256]).then_inc(tile_free, 1)
                after_unit("fox_v", i, i, TILE0["fox_v"] + 4 * i + 4)
            t = TILE0["fox_f"]
            act.wait_ge(tile_ready, t + 1)
            act.wait_ge(gate_in, 16)
            nc.scalar.activation(FG[:, 0, :], bank[t % 4][:, :], ACT.Identity, bias=BF[:, 0:1]).then_inc(tile_free, 1)
            act.wait_ge(tile_free, t + 1)
            nc.scalar.activation(FG[:, 1, :], FG[:, 0, :], ACT.Abs).then_inc(f_act, 1)
            act.wait_ge(f_act, 1)
            nc.scalar.activation(FG[:, 1, :], FG[:, 1, :], ACT.Exp, scale=-1.0).then_inc(f_act, 1)
            act.wait_ge(f_act, 2)
            nc.scalar.activation(FG[:, 1, :], FG[:, 1, :], ACT.Ln, bias=EPS[:, 2:3]).then_inc(f_act, 1)
            after_unit("fox_f", 0, 0, t + 1)
            for i in range(2):
                for k in range(2):
                    t = TILE0["fox_u"] + 2 * i + k
                    act.wait_ge(tile_ready, t + 1)
                    copy(UF[:, 2 * i + k, :], bank[t % 4][:, :]).then_inc(tile_free, 1)
                after_unit("fox_u", i, i, TILE0["fox_u"] + 2 * i + 2)
            act.wait_ge(f_mm, 1)
            for h in range(FOXH):
                act.wait_ge(f_mm, h + 2)
                copy(FB[:, h, :], bank[5 + h % 2][:, :], scale=-8.0).then_inc(f_act, 1)
            for g in range(4):
                act.wait_ge(pool_dve, POOL_DONE[g])
                copy(PLH[:, g, :], PW[:, 0, :]).then_inc(pool_hi, 1)
            for g in range(4):
                t = TILE0["fox_pool"] + g
                act.wait_ge(tile_ready, t + 1)
                sc = COLS["pool_scale"] + g
                nc.scalar.activation(UF[:, g, :], bank[t % 4][:, :], ACT.Copy, scale=COL[:, sc:sc + 1]).then_inc(tile_free, 1)
                act.wait_ge(tile_free, t + 1)
                copy(XH[:, 4 + g, :], UF[:, g, :]).then_inc(x_hi, 1)
            after_unit("fox_pool", 0, 0, TILE0["fox_pool"] + 4)
            attention("fox", 2, 4, 0.125, o_hi("fox_o"))
            wide_units("fox_o", nothing)
            rms("rms2", lambda c: (tile_free, TILE0["fox_o"] + c + 1), bank[7], G2, MODC[:, 24:32], True)
            hidden(2)
            rms("rms3", lambda c: (y_free, DC * 2 + c + 1), bank[1], COL[:, COLS["final"]:COLS["final"] + 8], None, False)
            for n in range(8):
                act.wait_ge(f_mm, 9 + n + 1)
                copy(ON[:, n // 2, 512 * (n % 2):512 * (n % 2) + 512], bank[4 + n % 4][:, :]).then_inc(out_ready, 1)

        @block.vector
        def _(dve):
            for s in (max_done, negmax_done, rsum_done, probs_ready, comb_done):
                dve.sem_inc(s, 4)
            nc.vector.memset(VR[:, :, :], 0.0).then_inc(cols_done, 1)
            for k, value in enumerate((LN_EPS, RMS_EPS, 1.0)):
                nc.vector.memset(EPS[:, k:k + 1], value).then_inc(eps_done, 1)
            nc.vector.memset(BF[:, :], 0.0).then_inc(eps_done, 1)
            for u in range(2):
                split_lo(dve, u, u)
            for c in range(8):
                t = TILE0["x_in"] + c
                dve.wait_ge(tile_free, t + 1)
                nc.vector.tensor_tensor(XL[:, c, :], XT[:, c, :], f32(XH[:, c, :]), ALU.subtract).then_inc(x_split, 1)
            two_pi = 2.0 * np.pi
            c1 = float(np.float32(6.28125))
            rest = np.array(two_pi - c1, np.float32).view(np.uint32) & np.uint32(0xFFFFF000)
            c2 = float(rest.view(np.float32))
            c3 = float(np.float32(two_pi - c1 - c2))
            magic = float(1.5 * 2 ** 23)
            edge = 3.1415925
            n = [0]

            def link(ins):
                n[0] += 1
                ins.then_inc(trig, 1)
                dve.wait_ge(trig, n[0])
            dve.wait_ge(pos_in, 16)
            dve.wait_ge(small_in, 32)
            link(nc.vector.tensor_copy(TRN[:, :], POSI[:, :]))
            link(nc.vector.tensor_scalar(ANG[:, :], TRN[:, :], KC[:, K_FREQ:K_FREQ + 1], None, ALU.mult))
            for k in range(2):
                nc.vector.tensor_scalar(TRN[:, :], ANG[:, :], float(1 / two_pi), 0.25 * k, ALU.mult, ALU.add).then_inc(rel_dve, 1)
                dve.wait_ge(rel_dve, 6 * k + 1)
                nc.vector.tensor_scalar(TRN[:, :], TRN[:, :], magic, None, ALU.add).then_inc(rel_dve, 1)
                dve.wait_ge(rel_dve, 6 * k + 2)
                nc.vector.tensor_scalar(TRN[:, :], TRN[:, :], -magic, None, ALU.add).then_inc(rel_dve, 1)
                dve.wait_ge(rel_dve, 6 * k + 3)
                nc.vector.scalar_tensor_tensor(out=RT[:, k, :], in0=TRN[:, :], scalar=-c1, in1=ANG[:, :],
                                               op0=ALU.mult, op1=ALU.add).then_inc(rel_dve, 1)
                dve.wait_ge(rel_dve, 6 * k + 4)
                nc.vector.scalar_tensor_tensor(out=RT[:, k, :], in0=TRN[:, :], scalar=-c2, in1=RT[:, k, :],
                                               op0=ALU.mult, op1=ALU.add).then_inc(rel_dve, 1)
                dve.wait_ge(rel_dve, 6 * k + 5)
                nc.vector.scalar_tensor_tensor(out=RT[:, k, :], in0=TRN[:, :], scalar=-c3, in1=RT[:, k, :],
                                               op0=ALU.mult, op1=ALU.add).then_inc(rel_dve, 1)
                dve.wait_ge(rel_dve, 6 * k + 6)
                link(nc.vector.tensor_scalar(RT[:, k, :], RT[:, k, :], 0.5 * np.pi * k, edge, ALU.add, ALU.min))
                link(nc.vector.tensor_scalar(RT[:, k, :], RT[:, k, :], -edge, None, ALU.max))
            assert n[0] == 6
            dve.wait_ge(c_hi, 1)
            nc.vector.tensor_tensor(CAL[:, :], CA[:, :], f32(CAH[:, :]), ALU.subtract).then_inc(mod_hi, 1)

            for i in range(4):
                next_lo(dve, "mla_in", i, i)
            for q in range(2):
                dve.wait_ge(std_done, q + 1)
                nc.vector.reciprocal(RQ[:, q, :], RQ[:, q, :]).then_inc(c_scaled, 1)
            for c in range(6):
                if c in (0, 4):
                    dve.wait_ge(c_scaled, 2)
                nc.vector.tensor_tensor(CR[:, c, :], CR[:, c, :], RQ[:, c // 4, :], ALU.mult).then_inc(c_scaled, 1)
            for c in range(6):
                dve.wait_ge(c_affine, 6 + 2 * c + 2)
                nc.vector.tensor_tensor(CL[:, c, :], CR[:, c, :], f32(CH[:, c, :]), ALU.subtract).then_inc(c_split, 1)
            for i in range(4):
                next_lo(dve, "mla_uq", i, i)
            dve.wait_ge(trig_act, 1)
            for r in range(5):
                x = bank[6][:, :] if r == 0 else QR[:, r - 1, :]
                dve.wait_ge(rope_mm, 6 + r + 1)
                nc.vector.tensor_tensor(RP[:, 0, :], x, COS[:, :], ALU.mult).then_inc(rope_dve, 1)
                nc.vector.tensor_tensor(RP[:, 1, :], bank[4 + r % 2][:, :], SIN[:, :], ALU.mult).then_inc(rope_dve, 1)
                dve.wait_ge(rope_dve, 3 * r + 2)
                nc.vector.tensor_tensor(KR[:, :] if r == 0 else x, RP[:, 0, :], RP[:, 1, :], ALU.add).then_inc(rope_dve, 1)
                dve.wait_ge(rope_dve, 3 * r + 3)
            for i in range(2):
                next_lo(dve, "mla_ukv", i, i)


            def attention(name, groups, heads, scale, bias, out_tile):
                steps = 4 * heads
                s0 = STEP0[name]
                xa = name[:2] == "xa"
                with dve.Fori(0, groups) as g:
                    def maxima(i):
                        w = MEM if xa else P * (i % 4) + P
                        pb = PBUF[name][:, i % 4, 0:w]
                        dve.wait_ge(turned, g * steps + (s0 + i - 3))
                        in1 = bias(g, i, pb)
                        dve.wait_ge(logits_ready, g * steps + (s0 + i + 1))
                        dve.sem_inc(logits_seen, 1)
                        nc.vector.tensor_tensor_reduce(pb, bank[i % 4][:, 0:w], in1, 1.0, TAKEN, ALU.add, ALU.max,
                                                       MX[:, i % 4:i % 4 + 1]).then_inc(max_done, 1)
                        dve.wait_ge(max_done, g * steps + (s0 + i + 1))
                        nc.vector.tensor_scalar(NM[:, i % 4:i % 4 + 1], MX[:, i % 4:i % 4 + 1], -scale, None,
                                                ALU.mult).then_inc(negmax_done, 1)

                    def normalise(i):
                        w = MEM if xa else P * (i % 4) + P
                        pb = PBUF[name][:, i % 4, 0:w]
                        dve.wait_ge(exp_done, g * steps + (s0 + i + 1))
                        nc.vector.reciprocal(RI[:, i % 4:i % 4 + 1], RS[:, i % 4:i % 4 + 1]).then_inc(rsum_done, 1)
                        dve.wait_ge(rsum_done, g * steps + (s0 + i + 1))
                        nc.vector.tensor_scalar(pb, pb, RI[:, i % 4:i % 4 + 1], None, ALU.mult).then_inc(probs_ready, 1)

                    def outs(i):
                        if out_tile is None:
                            return
                        if xa:
                            if i == 3:
                                for d in range(2):
                                    out_tile(g, d)
                        elif i % 8 == 7:
                            out_tile(g, i // 8)
                    for i in range(steps):
                        maxima(i)
                        if i >= 1:
                            normalise(i - 1)
                        if i >= 6:
                            outs(i - 6)
                    normalise(steps - 1)
                    for i in range(max(0, steps - 6), steps):
                        outs(i)

            def o_lo(fill, hi0, c0=0):
                def out_tile(g, k):
                    dve.wait_ge(x_hi, g * 2 + (hi0 + k + 1))
                    c = g * 2 + (k + c0)
                    nc.vector.tensor_tensor(XL[:, bass.ds(c, 1), :], bank[6 + k][:, :], f32(XH[:, bass.ds(c, 1), :]),
                                            ALU.subtract).then_inc(x_split, 1)
                return out_tile

            def x_hi0(fill):
                return FILL0[fill] - 8

            attention("mla", 4, 4, MLA_SCALE, lambda g, i, pb: cm(i % 4), o_lo("mla_o", x_hi0("mla_o")))

            def proj_units(stage, gain=None):
                def unit(i, j):
                    for k in range(2):
                        t = i * 2 + (TILE0[stage] + k)
                        b = bank[(TILE0[stage] + 2 * j + k) % 4]
                        c = bass.ds(i * 2 + k, 1)
                        dve.wait_ge(tile_ready, t + 1)
                        if gain is None:
                            nc.vector.scalar_tensor_tensor(out=ZB[:, c, :], in0=XT[:, c, :], scalar=ALPHA, in1=b[:, :],
                                                           op0=ALU.mult, op1=ALU.add).then_inc(tile_free, 1)
                        else:
                            nc.vector.scalar_tensor_tensor(out=XT[:, c, :], in0=b[:, :],
                                                           scalar=MODC[:, bass.ds(i * 2 + (gain + k), 1)], in1=XT[:, c, :],
                                                           op0=ALU.mult, op1=ALU.add).then_inc(tile_free, 1)
                    next_lo(dve, stage, i, j)
                by_pairs(dve, 4, unit)

            def norm(name, src, mean_bank, ready):
                k = NORM_I[name]
                if mean_bank is not None:
                    dve.wait_ge(mean_ready, k + 1)
                    for c in range(DC):
                        dve.wait_ge(*ready(c))
                        nc.vector.tensor_tensor(ZB[:, c, :], ZB[:, c, :], mean_bank[:, :], ALU.subtract).then_inc(centred, 1)
                dve.wait_ge(std_done, k + 3)
                nc.vector.reciprocal(RSTD[:, :], STD[:, :]).then_inc(rstd_done, 1)
                dve.wait_ge(rstd_done, k + 1)
                for c in range(DC):
                    nc.vector.tensor_tensor(ZB[:, c, :], src[:, c, :], RSTD[:, :], ALU.mult).then_inc(scaled, 1)

            def lows(fill, src):
                for c in range(DC):
                    dve.wait_ge(x_hi, x_hi0(fill) + c + 1)
                    nc.vector.tensor_tensor(XL[:, c, :], src[:, c, :], f32(XH[:, c, :]), ALU.subtract).then_inc(x_split, 1)

            def ln(idx, ready, mean_bank, low=True):
                norm(f"ln{idx}", ZB, mean_bank, ready)
                if low:
                    lows(f"ln{idx}", XT)

            def ln_proj(idx, stage):
                proj_units(stage)
                ln(idx, lambda c: (tile_free, TILE0[stage] + c + 1), bank[6])

            ln_proj(0, "mla_o")

            def cross_attention(layer):
                for c in range(DC):
                    t = TILE0[f"mem{layer}"] + c
                    dve.wait_ge(mod_done, 8 * layer + c + 1)
                    nc.vector.tensor_tensor(ML[:, c, :], bank[t % 4][:, 0:MEM], f32(MH[:, c, :]),
                                            ALU.subtract).then_inc(tile_free, 1)
                by_pairs(dve, 8, lambda i, j: next_lo(dve, f"xa_kv{layer}", i, j))
                by_pairs(dve, 4, lambda i, j: next_lo(dve, f"xa_q{layer}", i, j))
                attention(f"xa{layer}", 4, 1, (D // 4) ** -0.5, lambda g, i, pb: KC[:, K_CM:K_CM + MEM],
                          o_lo(f"xa{layer}_o", x_hi0(f"xa{layer}_o")))
                ln_proj(3 * layer + 1, f"xa_o{layer}")

            def hidden(f):
                name = f"ffn_in{f}"

                def unit(i, j):
                    b0, b1 = bank[(TILE0[name] + 2 * j) % 4], bank[(TILE0[name] + 2 * j + 1) % 4]
                    t = i * 2 + TILE0[name]
                    if f < 2:
                        dve.wait_ge(tile_ready, t + 2)
                        dve.wait_ge(silu_done, i + (FC * f + 1))
                        nc.vector.tensor_tensor(HF[:, j, :], SG[:, j, :], b1[:, :], ALU.mult).then_inc(tile_free, 2)
                    else:
                        for n, b in enumerate((b0, b1)):
                            y = (SG, HF)[n]
                            dve.wait_ge(tap_done, i * 2 + (n + 1))
                            for m, tap in enumerate(("conv_w1", "conv_w0")):
                                s = m + 1
                                if m:
                                    dve.wait_ge(conv_acc, i * 4 + (2 * n + 1))
                                nc.vector.scalar_tensor_tensor(
                                    out=y[:, j, s:S], in0=b[:, 0:S - s], scalar=COL[:, bass.ds(i + (COLS[tap] + FC * n), 1)],
                                    in1=y[:, j, s:S], op0=ALU.mult, op1=ALU.add).then_inc(conv_acc, 1)
                        dve.wait_ge(silu_done, i + (FC * f + 1))
                        dve.wait_ge(conv_acc, i * 4 + 4)
                        nc.vector.tensor_tensor(HF[:, j, :], SG[:, j, :], HF[:, j, :], ALU.mult).then_inc(tile_free, 2)
                    dve.wait_ge(hid_hi, i + (FC * f + 1))
                    nc.vector.tensor_tensor(HL[:, bass.ds(i, 1), :], HF[:, j, :], f32(HH[:, bass.ds(i, 1), :]),
                                            ALU.subtract).then_inc(hid_split, 1)
                    next_lo(dve, name, i, j)
                by_pairs(dve, FC, unit)
                down = f"ffn_down{f}"
                next_lo(dve, down, 0, 0)
                with dve.Fori(0, 4) as pair:
                    for j in range(2):
                        next_lo(dve, down, pair * 2 + (1 + j), 1 + j)
                next_lo(dve, down, 9, 9)
                next_lo(dve, down, 10, 10)
                for c in range(DC):
                    dve.wait_ge(y_ready, DC * f + c + 1)
                    if f < 2:
                        nc.vector.scalar_tensor_tensor(out=ZB[:, c, :], in0=XT[:, c, :], scalar=ALPHA, in1=bank[c][:, :],
                                                       op0=ALU.mult, op1=ALU.add).then_inc(y_free, 1)
                    else:
                        nc.vector.scalar_tensor_tensor(out=XT[:, c, :], in0=bank[c][:, :], scalar=MODC[:, 40 + c:41 + c],
                                                       in1=XT[:, c, :], op0=ALU.mult, op1=ALU.add).then_inc(y_free, 1)

            def ln_down(idx, f, low=True):
                ln(idx, lambda c: (y_free, DC * f + c + 1), bank[0], low)

            cross_attention(0)
            hidden(0)
            ln_down(2, 0)

            by_pairs(dve, 4, lambda i, j: next_lo(dve, "dsa_q", i, j))
            for name in ("dsa_k", "dsa_v"):
                next_lo(dve, name, 0, 0)
            for i in range(2):
                next_lo(dve, "dsa_qi", i, i)
            next_lo(dve, "dsa_ki", 0, 0)
            boff = [0, 128, 384, 768]
            dve.wait_ge(tile_free, TILE0["dsa_ki"] + 6)
            dve.wait_ge(tile_ready, TILE0["dsa_ki"] + 6)
            for i in range(NQ * IDXH):
                qb, h = divmod(i, IDXH)
                w = P * qb + P
                mk = MK[:, boff[qb]:boff[qb] + w]
                dve.wait_ge(idx_relu, i + 1)
                if h == 0:
                    nc.vector.scalar_tensor_tensor(out=mk, in0=RL[:, i % 2, 0:w], scalar=WIX[:, qb, h:h + 1], in1=cm(qb),
                                                   op0=ALU.mult, op1=ALU.add).then_inc(idx_acc, 1)
                else:
                    dve.wait_ge(idx_acc, i)
                    nc.vector.scalar_tensor_tensor(out=mk, in0=RL[:, i % 2, 0:w], scalar=WIX[:, qb, h:h + 1], in1=mk,
                                                   op0=ALU.mult, op1=ALU.add).then_inc(idx_acc, 1)
            dve.wait_ge(idx_acc, NQ * IDXH)
            n_top = [0]

            def top(ins):
                n_top[0] += 1
                ins.then_inc(topk, 1)
                dve.wait_ge(topk, n_top[0])
            top(nc.vector.tensor_copy(MK[:, 0:P], cm(0)))
            for qb in range(1, NQ):
                w = P * qb + P
                mk = MK[:, boff[qb]:boff[qb] + w]
                for r in range(TOPK // 8):
                    top(nc.vector.max(M8[:, :], mk))
                    top(nc.vector.match_replace(mk, M8[:, :], mk, TAKEN))
                top(nc.vector.tensor_scalar(mk, mk, TAKEN / 2, NEG, ALU.is_gt, ALU.mult))
                top(nc.vector.tensor_tensor(mk, mk, cm(qb), ALU.add))
            dve.wait_ge(rel_in, 16 * 7)
            n_rel = [12]

            def rel(ins):
                n_rel[0] += 1
                ins.then_inc(rel_dve, 1)
                dve.wait_ge(rel_dve, n_rel[0])
            rel(nc.vector.tensor_copy(PK[:, :], PI[:, :]))
            rel(nc.vector.tensor_scalar(PQ[:, :], PK[:, :], KC[0:96, K_THR:K_THR + 1], None, ALU.subtract))
            rel(nc.vector.tensor_tensor(DW[:, 0, :], RB[:, 0, :], RB[:, 1, :], ALU.subtract))
            for k in range(3):
                rel(nc.vector.tensor_copy(DB[:, k, :], DW[:, k, :]))
                rel(nc.vector.tensor_tensor(DW[:, k + 1, :], DW[:, k, :], DB[:, k, :], ALU.subtract))
            for k in range(3):
                rel(nc.vector.tensor_copy(DEL[32 * k:32 * k + 32, :], DB[32 * k:32 * k + 32, k, :]))
            assert n_rel[0] == REL_N
            dve.sem_inc(bias_free, 4)
            dve.wait_ge(v_moved, 1)
            for kb in range(NQ):
                n = NQ - kb
                with dve.Fori(0, 4) as kg:
                    for k in range(32):
                        key = kg * 32 + (P * kb + k)
                        dve.wait_ge(step_used, key + 1)
                        nc.vector.tensor_scalar(ST[:, k % 8, P * kb:S], PQ[:, P * kb:S], PK[:, bass.ds(key, 1)], None,
                                                ALU.is_ge).then_inc(step_done, 1)
                    dve.wait_ge(step_used, kg * 32 + (P * kb + 32 + 8))
                    for qb in range(kb, NQ):
                        w = P * qb + P
                        k0 = kg * 32 + P * kb
                        src = bank[qb][:, :].rearrange("q (k h) -> q h k", h=HEADS)
                        m = MK[:, bass.ds(k0 + boff[qb], 32)].unsqueeze(1).broadcast_to((P, HEADS, 32))
                        nc.vector.tensor_tensor(BI[:, :, bass.ds(k0 + boff[qb], 32)], src, m, ALU.add).then_inc(bias_free, 1)

            def dsa_bias(g, i, pb):
                dve.wait_ge(bias_staged, g * 16 + (i + 1))
                return pb
            attention("dsa", 4, 4, 1.0, dsa_bias, None)
            lows("dsa_o", QD)
            ln_proj(3, "dsa_o")
            cross_attention(1)
            hidden(1)
            ln_down(5, 1, low=False)

            with dve.Fori(0, 6) as four:
                for j in range(4):
                    i = four * 4 + j
                    t = i + TILE0["mod"]
                    dve.wait_ge(mod_done, i * 2 + 16)
                    dve.wait_ge(tile_ready, t + 1)
                    for k in range(2):
                        ins = nc.vector.tensor_tensor(PW[:, k, 0:P], bank[(TILE0["mod"] + j) % 4][:, P * k:P * k + P], IDN, ALU.mult)
                        if k == 0:
                            ins.then_inc(mod_done, 1)
                        else:
                            ins.then_inc(tile_free, 1)
                    dve.wait_ge(mod_done, i * 2 + 17)
                    dve.wait_ge(tile_free, t + 1)
                    nc.vector.tensor_reduce(MODR[:, bass.ds(i * 2, 2)], PW[:, 0:2, 0:P], AXX, ALU.add).then_inc(mod_done, 1)
                    split_lo(dve, i + (UNIT0["mod"] + 2), (UNIT0["mod"] + j) % 2)
            dve.wait_ge(mod_done, 16 + 48)
            nc.vector.tensor_tensor(MODC[:, :], MODR[:, :], COL[:, COLS["mod_b"]:COLS["mod_b"] + 48], ALU.add).then_inc(mod_done, 1)
            dve.wait_ge(mod_done, 65)
            for k, (gain, sc, g) in enumerate(((G1, 8, "norm1"), (G2, 32, "norm2"))):
                nc.vector.scalar_tensor_tensor(out=gain[:, :], in0=MODC[:, sc:sc + 8], scalar=1.0,
                                               in1=COL[:, COLS[g]:COLS[g] + 8], op0=ALU.add, op1=ALU.mult).then_inc(mod_done, 1)
            dve.wait_ge(mod_done, 67)
            norm("rms1", XT, None, None)
            lows("rms1", ZB)
            by_pairs(dve, 4, lambda i, j: next_lo(dve, "fox_qk", i, j))
            for i in range(2):
                next_lo(dve, "fox_v", i, i)
            next_lo(dve, "fox_f", 0, 0)
            for i in range(2):
                next_lo(dve, "fox_u", i, i)
            dve.wait_ge(tile_free, TILE0["fox_f"] + 1)
            dve.wait_ge(f_act, 3)
            nc.vector.scalar_tensor_tensor(out=FG[:, 2, :], in0=FG[:, 0, :], scalar=0.0, in1=FG[:, 1, :],
                                           op0=ALU.min, op1=ALU.subtract).then_inc(f_dve, 1)
            dve.wait_ge(f_dve, 1)
            nc.vector.memset(FG[:, 1, :], 1.0).then_inc(f_dve, 1)
            dve.wait_ge(f_dve, 2)
            nc.vector.tensor_tensor_scan(FG[:, 3, :], FG[:, 1, :], FG[:, 2, :], 0.0, ALU.mult, ALU.add).then_inc(f_dve, 2)
            dve.wait_ge(f_mm, 1)
            nc.vector.tensor_scalar(FQ[:, :, :], bank[7][:, :].rearrange("p (b r h) -> p b r h", b=NQ, h=FOXH)[:, :, 0, :],
                                    8.0, None, ALU.mult).then_inc(f_dve, 1)
            n_pool = [0]

            def pool(ins):
                n_pool[0] += 1
                ins.then_inc(pool_dve, 1)
                dve.wait_ge(pool_dve, n_pool[0])
            for g, w in enumerate(WINDOWS):
                u = UF[:, g, :]
                dve.wait_ge(tile_free, TILE0["fox_u"] + g + 1)
                if g:
                    dve.wait_ge(pool_hi, g)
                src = u
                for d in range(g + 1):
                    dst = PW[:, 1 + d % 2, :]
                    s = 1 << d
                    pool(nc.vector.tensor_copy(dst[:, 0:s], src[:, 0:s]))
                    pool(nc.vector.tensor_tensor(dst[:, s:S], src[:, s:S], src[:, 0:S - s], ALU.add))
                    src = dst
                pool(nc.vector.tensor_tensor(PW[:, 0, 0:16], src[:, 0:16], KC[:, K_CNT + 16 * g:K_CNT + 16 * g + 16], ALU.mult))
                nc.vector.tensor_tensor(PW[:, 0, 0:16], PW[:, 0, 0:16], u[:, 0:16], ALU.subtract)
                pool(nc.vector.scalar_tensor_tensor(out=PW[:, 0, 16:S], in0=src[:, 16:S], scalar=1.0 / w, in1=u[:, 16:S],
                                                    op0=ALU.mult, op1=ALU.subtract))
                dve.wait_ge(pool_hi, g + 1)
                nc.vector.tensor_tensor(PLL[:, g, :], PW[:, 0, :], f32(PLH[:, g, :]), ALU.subtract).then_inc(pool_split, 1)
            for g in range(4):
                dve.wait_ge(x_hi, x_hi0("fox_o") + g + 1)
                nc.vector.tensor_tensor(XL[:, 4 + g, :], UF[:, g, :], f32(XH[:, 4 + g, :]), ALU.subtract).then_inc(x_split, 1)
            next_lo(dve, "fox_pool", 0, 0)
            dve.wait_ge(f_act, 11)
            dve.wait_ge(f_dve, 5)

            def fox_bias(g, i, pb):
                hh, qb = divmod(i, 4)
                w = P * qb + P
                h = g * 4 + hh
                nc.vector.scalar_tensor_tensor(out=pb, in0=FB[:, bass.ds(h, 1), 0:w], scalar=FQ[:, qb, bass.ds(h, 1)],
                                               in1=cm(qb), op0=ALU.add, op1=ALU.add).then_inc(comb_done, 1)
                dve.wait_ge(comb_done, g * 16 + (4 + i + 1))
                return pb
            attention("fox", 2, 4, 0.125, fox_bias, o_lo("fox_o", x_hi0("fox_o") + 4))
            proj_units("fox_o", gain=16)
            norm("rms2", XT, None, None)
            lows("rms2", ZB)
            hidden(2)
            norm("rms3", XT, None, None)

        @block.gpsimd
        def _(pool):
            pool.dma_start(POSI[:, :], A["positions"].broadcast_to((P, S))).then_inc(pos_in, 16)
            pool.wait_ge(cols_done, 1)
            ROWS = [(0, COLS["ln_g"], A["ln_g"].rearrange("a b (c p) -> (a b c) p", p=P)),
                    (0, COLS["ln_b"], A["ln_b"].rearrange("a b (c p) -> (a b c) p", p=P)),
                    (0, COLS["q_norm"], A["mla_q_norm"].rearrange("a (c p) -> (a c) p", p=P)),
                    (0, COLS["kv_norm"], A["mla_kv_norm"].rearrange("a (c p) -> (a c) p", p=P)),
                    (0, COLS["norm1"], A["norm1_g_2"].rearrange("a (c p) -> (a c) p", p=P)),
                    (0, COLS["norm2"], A["norm2_g_2"].rearrange("a (c p) -> (a c) p", p=P)),
                    (0, COLS["final"], A["final_g_2"].rearrange("(c p) -> c p", p=P)),
                    (1, COLS["pool_scale"], A["pool_scale_2"].rearrange("a (c p) -> (a c) p", p=P)),
                    (1, COLS["conv_b"], A["ffn_conv_b_2"].rearrange("a (c p) -> (a c) p", p=P)),
                    (1, COLS["mod_b"], A["mod_b_2"].rearrange("a (c p) -> (a c) p", p=P)),
                    (1, COLS["c"], A["c_2"].rearrange("a (c p) -> (a c) p", p=P)),
                    (2, COLS["conv_w0"], A["ffn_conv_w_2"][0, 0:1].rearrange("a (c p) -> (a c) p", p=P)),
                    (2, COLS["conv_w1"], A["ffn_conv_w_2"][0, 1:2].rearrange("a (c p) -> (a c) p", p=P)),
                    (3, COLS["conv_w2"], A["ffn_conv_w_2"][0, 2:3].rearrange("a (c p) -> (a c) p", p=P))]
            for k, col, src in ROWS:
                p0 = col - P * k
                pool.dma_start(VR[p0:p0 + src.shape[0], k, :], src).then_inc(rows_in, 16)
            pool.wait_ge(eps_done, 4)
            pool.dma_start(BF[0:FOXH, :], A["b_f_2"].rearrange("a h -> h a")).then_inc(gate_in, 16)

            def tc(dst, src):
                return nc.gpsimd.tensor_copy(dst, src)

            def stage_group(name, groups, steps, items):
                def group(g, first):
                    for dst, src, freed_by, at_step in items:
                        if not first:
                            pool.wait_ge(freed_by, g * steps + (STEP0[name] - steps + at_step))
                        tc(dst, src(g)).then_inc(staged, 1)
                group(0, True)
                with pool.Fori(1, groups) as g:
                    group(g, False)

            def tiles(buf, per, k):
                return lambda g: buf[:, bass.ds(g * per + k, 1), :]

            pool.wait_ge(rope_dve, 15)
            pool.wait_ge(tile_free, TILE0["mla_o"])
            stage_group("mla", 4, 16, [
                (Q_M[:, 0, :], tiles(QN, 2, 0), logits_ready, 8), (K_M[:, 0, :], tiles(KN, 2, 0), logits_ready, 8),
                (Q_M[:, 1, :], tiles(QN, 2, 1), logits_ready, 16), (K_M[:, 1, :], tiles(KN, 2, 1), logits_ready, 16),
                (Q_M[:, 2, :], tiles(QR, 1, 0), logits_ready, 16),
                (V_M[:, :, 0:P], lambda g: VM[:, :, bass.ds(g * 256, P)], av_done, 8),
                (V_M[:, :, P:256], lambda g: VM[:, :, bass.ds(g * 256 + P, P)], av_done, 16)])

            def cross_attention(layer):
                name = f"xa{layer}"
                pool.dma_start(MN[:, :, :], A["mem"][0].rearrange("(b p) d -> p b d", p=P)).then_inc(mem_in, 16)
                pool.wait_ge(tile_free, TILE0[f"xa_o{layer}"])
                stage_group(name, 4, 4, [
                    (Q_X[:, 0, :], tiles(QX, 2, 0), logits_ready, 4), (Q_X[:, 1, :], tiles(QX, 2, 1), logits_ready, 4),
                    (V_X[:, :, :], lambda g: VX[:, :, bass.ds(g * 256, 256)], av_done, 4)])

            pool.wait_ge(av_done, STEP0["mla"] + 64)
            cross_attention(0)
            pool.wait_ge(tile_ready, TILE0["dsa_ki"] + 6)
            pool.dma_start(PI[:, :], A["positions"].broadcast_to((96, S))).then_inc(rel_in, 16)
            nc.gpsimd.memset(RB[:, :, :], 0.0).then_inc(pool_zero, 1)
            pool.wait_ge(pool_zero, 1)
            for k in range(3):
                pool.dma_start(RB[32 * k:32 * k + 32, 0, :], A["rel_bias"]).then_inc(rel_in, 16)
                pool.dma_start(RB[32 * k + 1:32 * k + 32, 1, :], A["rel_bias"][0:31, :]).then_inc(rel_in, 16)
            pool.wait_ge(bias_free, 44)
            pool.wait_ge(v_moved, 1)
            dsa_items = [
                (Q_D[:, 0, :], tiles(QD, 2, 0), logits_ready, 8), (Q_D[:, 1, :], tiles(QD, 2, 1), logits_ready, 16),
                (K_D[:, :], tiles(KD, 1, 0), logits_ready, 16),
                (V_D[:, :, :], lambda g: VK[:, :, bass.ds(g * 64, 64)], av_done, 16)]
            boff = [0, 128, 384, 768]

            def dsa_group(g, first):
                for n, (dst, src, freed_by, at_step) in enumerate(dsa_items):
                    if not first:
                        pool.wait_ge(freed_by, g * 16 + (STEP0["dsa"] - 16 + at_step))
                    tc(dst, src(g)).then_inc(staged, 1)
                for i in range(16):
                    hh, qb = divmod(i, 4)
                    w = P * qb + P
                    pool.wait_ge(turned, g * 16 + (STEP0["dsa"] + i - 3))
                    tc(PB_D[:, i % 4, 0:w], BI[:, bass.ds(g * 4 + hh, 1), boff[qb]:boff[qb] + w]).then_inc(bias_staged, 1)
            dsa_group(0, True)
            with pool.Fori(1, 4) as g:
                dsa_group(g, False)
            pool.wait_ge(av_done, STEP0["dsa"] + 64)
            cross_attention(1)
            pool.wait_ge(tile_ready, TILE0["fox_f"] + 1)
            pool.wait_ge(tile_free, TILE0["fox_o"])
            stage_group("fox", 2, 16, [
                (Q_F[:, 0, :], tiles(QF, 2, 0), logits_ready, 8), (K_F[:, 0, :], lambda g: QF[:, bass.ds(g * 2 + 4, 1), :], logits_ready, 8),
                (Q_F[:, 1, :], tiles(QF, 2, 1), logits_ready, 16), (K_F[:, 1, :], lambda g: QF[:, bass.ds(g * 2 + 5, 1), :], logits_ready, 16),
                (V_F[:, :, 0:P], lambda g: VF[:, :, bass.ds(g * 256, P)], av_done, 8),
                (V_F[:, :, P:256], lambda g: VF[:, :, bass.ds(g * 256 + P, P)], av_done, 16)])


_INS = ["x", "mem", "positions", "rel_bias", "mla_w_in", "mla_q_norm", "mla_w_uq", "mla_kv_norm", "mla_w_ukv", "mla_w_o",
        "dsa_w_in", "dsa_w_o", "xa_w_q", "xa_w_kv", "xa_w_o", "ffn_w_in", "ffn_w_down", "ln_g", "ln_b", "c_2", "mod_w_2",
        "mod_b_2", "norm1_g_2", "norm2_g_2", "w_in_2", "b_f_2", "pool_w_2", "pool_scale_2", "w_out_2", "ffn_up_2",
        "ffn_conv_w_2", "ffn_conv_b_2", "ffn_down_2", "final_g_2"]


def kernel(**inputs):
    import concourse.bacc as bacc
    from concourse.bass_utils import run_bass_kernel_spmd

    nc = bacc.Bacc("TRN2", target_bir_lowering=False, num_devices=1)
    arrays, A = {}, {}
    for name in _INS:
        a = np.ascontiguousarray(inputs[name])
        arrays[f"in_{name}"] = a
        A[name] = nc.dram_tensor(f"in_{name}", a.shape, mybir.dt.from_np(a.dtype), kind="ExternalInput").ap()
    k = shape_constants()
    arrays["in_shape_constants"] = k
    consts = nc.dram_tensor("in_shape_constants", k.shape, F32, kind="ExternalInput").ap()
    out = nc.dram_tensor("out", (1, S, D), F32, kind="ExternalOutput").ap()
    build_program(nc, A, consts, out)
    r = run_bass_kernel_spmd(nc, [arrays], core_ids=[0])
    return r.results[0]["out"]
```
